# Optimizing a Trainium2 kernel written in Bass

```python
import math
import jax, jax.numpy as jnp
from jax import lax
import numpy as np

D_MODEL = 1024
BATCH = 1
SEQ = 1024
DEPTH = 1
DEC_BATCH = 1
DEC_SEQ = 1024
PAST_LEN = 128

MIX_W = D_MODEL
POOL_W = MIX_W // 2
N_POOL = 4
POOL_GROUP = POOL_W // N_POOL
POOL_WINDOWS = (2, 4, 8, 16)
HEAD_DIM = 64
N_HEADS = (MIX_W - POOL_W) // HEAD_DIM
N_KV = 2
GROUP = N_HEADS // N_KV
Q_W = N_HEADS * HEAD_DIM
KV_W = N_KV * HEAD_DIM
IN_W = POOL_W + Q_W + 2 * KV_W
AX_DIM = HEAD_DIM // 2
ROPE_THETA = 10000.0
GRID_W = 64
Q_BLOCK = 128
D_FF = ((8 * D_MODEL // 3 + 255) // 256) * 256
PLE_DIM = 256
EPS = 1e-6

kernel_name = "hybrid_pool_gqa_axial_encoder"

def rms_norm(x, g):
    xf = x.astype(jnp.float32)
    y = xf * lax.rsqrt(jnp.mean(xf * xf, axis=-1, keepdims=True) + EPS)
    return (y * g.astype(jnp.float32)).astype(x.dtype)

def axial_rope_tables(seq):
    rows = seq // GRID_W
    row = jnp.repeat(jnp.arange(rows, dtype=jnp.float32), GRID_W)
    col = jnp.tile(jnp.arange(GRID_W, dtype=jnp.float32), rows)
    inv = 1.0 / (ROPE_THETA ** (jnp.arange(0, AX_DIM, 2, dtype=jnp.float32) / AX_DIM))
    ang = jnp.concatenate([row[:, None] * inv, col[:, None] * inv], axis=-1)
    return jnp.cos(ang), jnp.sin(ang)

def apply_rope(x, cos, sin):
    xf = x.astype(jnp.float32).reshape(*x.shape[:-1], HEAD_DIM // 2, 2)
    x0, x1 = xf[..., 0], xf[..., 1]
    c = cos[None, :, None, :]
    s = sin[None, :, None, :]
    out = jnp.stack([x0 * c - x1 * s, x0 * s + x1 * c], axis=-1)
    return out.reshape(x.shape).astype(x.dtype)

def pool_mixer(u, pool_w, pool_scale):
    B, S, _ = u.shape
    uf = u.astype(jnp.float32).reshape(B, S, N_POOL, POOL_GROUP)
    cs = jnp.concatenate([jnp.zeros((B, 1, N_POOL, POOL_GROUP), jnp.float32),
                          jnp.cumsum(uf, axis=1)], axis=1)
    t = jnp.arange(S)
    outs = []
    for g, w in enumerate(POOL_WINDOWS):
        lo = jnp.clip(t - w // 2, 0, S - 1)
        hi = jnp.clip(t + (w - 1 - w // 2), 0, S - 1)
        win = cs[:, hi + 1, g] - cs[:, lo, g]
        cnt = (hi - lo + 1).astype(jnp.float32)[None, :, None]
        outs.append(win / cnt - uf[:, :, g])
    m = jnp.stack(outs, axis=2).astype(u.dtype)
    y = jnp.einsum('bsgc,gcd->bsgd', m, pool_w)
    return y.reshape(B, S, POOL_W) * pool_scale

def block_attention(q, k, v):
    B, S, _, _ = q.shape
    nblk = S // Q_BLOCK
    scale = 1.0 / math.sqrt(HEAD_DIM)
    qb = q.reshape(B, nblk, Q_BLOCK, N_KV, GROUP, HEAD_DIM).transpose(1, 0, 2, 3, 4, 5)

    def one_block(qblk):
        s = jnp.einsum('bqkgd,bskd->bkgqs', qblk, k, preferred_element_type=jnp.float32) * scale
        p = jax.nn.softmax(s, axis=-1).astype(v.dtype)
        return jnp.einsum('bkgqs,bskd->bqkgd', p, v)

    o = lax.map(one_block, qb)
    return o.transpose(1, 0, 2, 3, 4, 5).reshape(B, S, Q_W)

def encoder_layer(x, p, ln_mix_pre, ln_mix_post, w_in, pool_w, pool_scale, q_norm, k_norm, w_out,
                  ln_ffn_pre, ln_ffn_post, w_gate, w_up, w_down, w_ple_proj, w_ple_gate, b_ple_gate):
    B, S, _ = x.shape
    cos, sin = axial_rope_tables(S)
    h = rms_norm(x, ln_mix_pre)
    z = h @ w_in
    u = z[..., :POOL_W]
    q = z[..., POOL_W:POOL_W + Q_W].reshape(B, S, N_HEADS, HEAD_DIM)
    k = z[..., POOL_W + Q_W:POOL_W + Q_W + KV_W].reshape(B, S, N_KV, HEAD_DIM)
    v = z[..., POOL_W + Q_W + KV_W:].reshape(B, S, N_KV, HEAD_DIM)
    pool_out = pool_mixer(u, pool_w, pool_scale)
    q = apply_rope(rms_norm(q, q_norm), cos, sin)
    k = apply_rope(rms_norm(k, k_norm), cos, sin)
    attn_out = block_attention(q, k, v)
    mix = jnp.concatenate([pool_out, attn_out], axis=-1) @ w_out
    x = x + rms_norm(mix, ln_mix_post)
    h = rms_norm(x, ln_ffn_pre)
    f = (jax.nn.silu(h @ w_gate) * (h @ w_up)) @ w_down
    x = x + rms_norm(f, ln_ffn_post)
    e = p @ w_ple_proj
    g = jax.nn.sigmoid((x @ w_ple_gate + b_ple_gate).astype(jnp.float32)).astype(x.dtype)
    return x + e * g

def setup_inputs(seed: int = 0) -> dict:
    key = jax.random.key(seed)
    ks = jax.random.split(key, 24)
    f32 = jnp.float32

    def nrm(k, shape, scale):
        return jax.random.normal(k, shape, f32) * scale

    def gain(k, shape):
        return 1.0 + 0.05 * jax.random.normal(k, shape, f32)

    return {
        "x_prompt": nrm(ks[0], (BATCH, SEQ, D_MODEL), 1.0),
        "x_sample": nrm(ks[1], (DEC_BATCH, DEC_SEQ, D_MODEL), 1.0),
        "p_prompt": nrm(ks[2], (DEPTH, BATCH, SEQ, PLE_DIM), 1.0),
        "p_sample": nrm(ks[3], (DEPTH, DEC_BATCH, DEC_SEQ, PLE_DIM), 1.0),
        "ln_mix_pre": gain(ks[4], (DEPTH, D_MODEL)),
        "ln_mix_post": gain(ks[5], (DEPTH, D_MODEL)),
        "w_in": nrm(ks[6], (DEPTH, D_MODEL, IN_W), D_MODEL ** -0.5),
        "pool_w": nrm(ks[7], (DEPTH, N_POOL, POOL_GROUP, POOL_GROUP), POOL_GROUP ** -0.5),
        "pool_scale": gain(ks[8], (DEPTH, POOL_W)),
        "q_norm": gain(ks[9], (DEPTH, HEAD_DIM)),
        "k_norm": gain(ks[10], (DEPTH, HEAD_DIM)),
        "w_out": nrm(ks[11], (DEPTH, MIX_W, D_MODEL), MIX_W ** -0.5),
        "ln_ffn_pre": gain(ks[12], (DEPTH, D_MODEL)),
        "ln_ffn_post": gain(ks[13], (DEPTH, D_MODEL)),
        "w_gate": nrm(ks[14], (DEPTH, D_MODEL, D_FF), D_MODEL ** -0.5),
        "w_up": nrm(ks[15], (DEPTH, D_MODEL, D_FF), D_MODEL ** -0.5),
        "w_down": nrm(ks[16], (DEPTH, D_FF, D_MODEL), D_FF ** -0.5),
        "w_ple_proj": nrm(ks[17], (DEPTH, PLE_DIM, D_MODEL), PLE_DIM ** -0.5),
        "w_ple_gate": nrm(ks[18], (DEPTH, D_MODEL, D_MODEL), D_MODEL ** -0.5),
        "b_ple_gate": nrm(ks[19], (DEPTH, D_MODEL), 0.02),
    }

def reference(x_prompt, x_sample, p_prompt, p_sample, ln_mix_pre, ln_mix_post, w_in, pool_w, pool_scale,
              q_norm, k_norm, w_out, ln_ffn_pre, ln_ffn_post, w_gate, w_up, w_down,
              w_ple_proj, w_ple_gate, b_ple_gate):
    def trunk(x, p):
        for i in range(DEPTH):
            x = encoder_layer(x, p[i], ln_mix_pre[i], ln_mix_post[i], w_in[i], pool_w[i], pool_scale[i],
                              q_norm[i], k_norm[i], w_out[i], ln_ffn_pre[i], ln_ffn_post[i],
                              w_gate[i], w_up[i], w_down[i], w_ple_proj[i], w_ple_gate[i], b_ple_gate[i])
        return x

    y_prompt = trunk(x_prompt, p_prompt)
    y_sample = trunk(x_sample, p_sample)
    return (y_prompt, y_sample)


_drawn_inputs = setup_inputs


def setup_inputs(seed=0):
    import zlib

    import numpy as np

    out = dict(_drawn_inputs(seed))
    spreads = {}
    factors = {'q_norm': 8.0, 'k_norm': 8.0, 'b_ple_gate': 29.053}
    for name, (base, spread) in spreads.items():
        noise = np.random.default_rng([zlib.crc32(name.encode()), seed]).standard_normal(out[name].shape)
        drawn = base * np.exp(spread * noise) if base else spread * noise
        out[name] = __import__('jax').numpy.asarray(drawn.astype(out[name].dtype))
    for name, factor in factors.items():
        out[name] = (out[name] * factor).astype(out[name].dtype)
    return out
```

```python
from contextlib import ExitStack, contextmanager

import numpy as np

import concourse.bass as bass
from concourse import mybir

F32 = mybir.dt.float32
F32R = mybir.dt.float32r
BF16 = mybir.dt.bfloat16
ALU = mybir.AluOpType
ACT = mybir.ActivationFunctionType
AX = mybir.AxisListType

P = 128
D = 1024
SEQ = 1024
NSEQ = 2
KT = D // P
NT = SEQ // P
POOL_W = 512
NPOOL = 4
WINDOWS = (2, 4, 8, 16)
PAD = 8
HD = 64
NH = 8
NKV = 2
GROUP = NH // NKV
Q_W = NH * HD
KV_W = NKV * HD
IN_W = POOL_W + Q_W + 2 * KV_W
GRID_W = 64
ROPE_THETA = 10000.0
DFF = 2816
PLE = 256
EPS = 1e-6

CH = 512
NCH = NSEQ * SEQ // CH
PARTS = (8, 8, 6)
PART0 = (0, 8, 16)
NHID = DFF // P
GU = tuple(n // 2 for n in PARTS)
DN = 2
NPLE = KT // 2
BODIES0 = sum(GU) + 3 * DN
BODIES = BODIES0 + NPLE


class Signal:

    def __init__(self, sem, start=0):
        self.sem, self.base, self.count = sem, start, 0

    def by(self, ins, n=1):
        ins.then_inc(self.sem, n)
        self.count += n

    @property
    def value(self):
        return self.base + self.count


@contextmanager
def repeat(engine, times, steps):
    kept = {s: (s.base, s.count) for s in steps}
    with engine.Fori(0, times) as i:
        for s, k in steps.items():
            s.base, s.count = kept[s][0] + kept[s][1] + i * k, 0
        yield i
        for s, k in steps.items():
            assert s.count == k, (s.sem, s.count, k)
    for s, k in steps.items():
        s.base, s.count = kept[s][0], kept[s][1] + times * k


def misc_schedule():
    order = [("q", 0, 0), ("q", 0, 1)]
    for h in range(NH):
        if h:
            order.append(("o", 2 * h - 2))
        if h + 1 < NH:
            order += [("q", h + 1, 0), ("q", h + 1, 1)]
        if h:
            order.append(("o", 2 * h - 1))
        order.append(("pool", h))
    order += [("o", 2 * NH - 2), ("o", 2 * NH - 1)]
    return {k: n for n, k in enumerate(order)}


MISC = misc_schedule()
NMISC = len(MISC)
NSTEP = NH * NT
NCONST = 10
POOL_STEPS = 2 * sum(n + 5 for n in range(NPOOL)) + 2 * NH
AB_STEPS = 13
V_STEPS = 136


def encoder_layer(nc, x, p, ident_d, cos_d, sin_d, edge_d, g_mix_pre, g_mix_post, w_in, pool_w,
                  pool_scale, q_norm, k_norm, w_out, g_ffn_pre, g_ffn_post, w_gate, w_up, w_down,
                  w_proj, w_pgate, b_pgate, y):
    x1t_d = nc.dram_tensor("x1_turned", (NCH, P, KT, CH), F32, kind="Internal").ap()
    h2t_d = nc.dram_tensor("h2_turned", (2, NCH, P, KT, CH), F32, kind="Internal").ap()

    top = ExitStack()
    with top:
        def sem(name):
            return top.enter_context(nc.semaphore(name))

        def sb(stack, name, shape, dt=F32):
            return stack.enter_context(nc.sbuf_tensor(name, shape, dt))

        ps = top.enter_context(nc.psum_tensor("ps", [P, 8, 512], F32))
        pair = lambda b: ps[:, b:b + 2, :].rearrange("p b n -> p (b n)")

        ident = sb(top, "ident", [P, P])
        ones = sb(top, "ones", [P, P], F32R)
        gpost2 = sb(top, "gpost2", [P, KT])
        bgate = sb(top, "bgate", [P, KT])
        small = sb(top, "small", [P, 16])
        eps = sb(top, "eps", [P, 2])

        consts_in = sem("consts_in")
        stage_done = sem("stage_done")
        stages = {}
        waited = {e: sem(f"waited_{n}") for n, e in enumerate(
            (nc.sync, nc.gpsimd, nc.tensor, nc.scalar, nc.vector))}

        def alone(e):
            e.sem_inc(waited[e], 1)

        def stage_end(e):
            g, n = stages[e]
            e.drain().then_inc(stage_done, 1)
            e.wait_ge(stage_done, 5 * (g * 3 + n + 1))
            alone(e)
            stages[e] = (g, n + 1)

        one = ExitStack()
        rope_c = sb(one, "rope_c", [P, NT, HD // 2])
        rope_s = sb(one, "rope_s", [P, NT, HD // 2])
        edge = sb(one, "edge", [P, NPOOL, 2, PAD])
        gqk = sb(one, "gqk", [P, 2, HD])
        gin = sb(one, "gin", [P, KT])
        pscale = sb(one, "pscale", [P, NPOOL])
        poolw = sb(one, "poolw", [P, 2, NPOOL, P], F32R)
        raw = sb(one, "raw", [P, 2, IN_W])
        heads = sb(one, "heads", [P, NT, NH, HD])
        keys = sb(one, "keys", [P, NKV, 2, SEQ], F32R)
        values = sb(one, "values", [P, NT, NKV, 2, HD], F32R)
        chan = sb(one, "chan", [P, NPOOL + 1, SEQ + 2 * PAD])
        negmax = sb(one, "negmax", [P, NSTEP])
        rowsum = sb(one, "rowsum", [P, NSTEP])
        recip = sb(one, "recip", [P, 4])

        s_a = ExitStack()
        win = sb(s_a, "win", [P, 2, KT, IN_W], F32R)
        ht = sb(s_a, "ht", [P, 2, 2, KT, P], F32R)
        xs_a = sb(s_a, "xs_a", [P, 2, D])
        hrow = sb(s_a, "hrow", [P, D])
        junk_a = sb(s_a, "junk_a", [P, D], BF16)
        utok = sb(s_a, "utok", [P, POOL_W])
        ktok = sb(s_a, "ktok", [P, NKV, HD])
        qtok = sb(s_a, "qtok", [P, NH, HD])
        tmp_a = sb(s_a, "tmp_a", [P, NH, HD])
        tmp_b = sb(s_a, "tmp_b", [P, NH, HD])
        kstack = sb(s_a, "kstack", [P, NKV, 4, HD])
        s_a.close()

        s_w = ExitStack()
        wout_a = sb(s_w, "wout_a", [P, 2, KT // 2, D], F32R)
        s_c = ExitStack()
        pt = sb(s_c, "pt", [P, 2, 2, KT, 4 * P], F32R)
        prob = sb(s_c, "prob", [P, 2, SEQ])
        qh = sb(s_c, "qh", [P, 2, 4, 2, HD])
        qs = sb(s_c, "qs", [P, 2, SEQ], F32R)
        ot = sb(s_c, "ot", [P, 4 * P])
        oparts = sb(s_c, "oparts", [P, 2, 4, HD])
        win_s = sb(s_c, "win_s", [P, 2, 528])
        mt_hl = sb(s_c, "mt_hl", [P, 2, 512], F32R)
        s_c.close()
        s_d = ExitStack()
        wout_b = sb(s_d, "wout_b", [P, 2, KT // 2, D], F32R)
        ct = sb(s_d, "ct", [P, 2, 2, KT, P], F32R)
        x1t = sb(s_d, "x1t", [P, KT, P])
        h2t = sb(s_d, "h2t", [P, 2, KT, P], F32R)
        xs_d = sb(s_d, "xs_d", [P, 2, D])
        mixn = sb(s_d, "mixn", [P, D])
        x1 = sb(s_d, "x1", [P, D])
        h2 = sb(s_d, "h2", [P, D])
        junk_d = sb(s_d, "junk_d", [P, D], BF16)
        gpost = sb(s_d, "gpost", [P, D])
        gffn = sb(s_d, "gffn", [P, D])
        s_d.close()
        s_w.close()
        one.close()

        two = ExitStack()
        h2c = sb(two, "h2c", [P, 2, KT, CH], F32R)
        ff = sb(two, "ff", [P, 2, max(PARTS), CH], F32R)
        ft = sb(two, "ft", [P, KT, CH])
        x2 = sb(two, "x2", [P, 2, KT, CH], F32R)
        rawb = sb(two, "rawb", [P, 2, 8 * 256])
        wb = sb(two, "wb", [P, 2, 2, 8 * 256], F32R)
        ptok = sb(two, "ptok", [P, 4, PLE])
        pturn = sb(two, "pturn", [P, 2, 2, CH], F32R)
        yrow = sb(two, "yrow", [P, 4, 256])
        gated = sb(two, "gated", [P, 2, CH])
        prod = sb(two, "prod", [P, 2, CH])
        xres = sb(two, "xres", [P, 2, 2, CH])
        sumsq = sb(two, "sumsq", [P, CH])
        sumhl = sb(two, "sumhl", [P, 2, CH], F32R)
        rnorm = sb(two, "rnorm", [P, CH])
        sqs = sb(two, "sqs", [P, 2, CH])
        two.close()

        S = {n: sem(n) for n in (
            "raw_in0", "raw_in1", "strip_hi", "strip_split", "xa_in0", "xa_in1", "x_sum", "x_root", "k_sums", "k_root", "q_sums", "q_root", "h_ready",
            "x_turned", "ht_hi", "ht_split", "kv_done", "u_done", "q_done", "v_hi", "k_raw",
            "v_split", "u_out", "q_out", "u_turned", "u_stored", "k_stack", "k_turned", "k_stored",
            "q_rope", "step_v", "step_a", "step_g", "pw_raw", "pw_hi", "pw_split",
            "score_done", "max_done", "exp_done", "p_turned", "p_hi", "p_split", "pv_done",
            "o_out", "misc_done", "misc_free", "qh_ready", "o_parts", "o_added", "m_ready",
            "xd_in0", "xd_in1", "gains_in", "a_turned", "c_hi", "c_split", "mix_c0", "mix_done",
            "m_sum", "m_root", "mix_read", "x1_ready", "x1_sum", "x1_root", "h2_ready", "x1_turned", "x1_out",
            "h2_turned", "h2_hi", "h2_out", "x1_stored", "h2_stored",
            "rawA", "rawB", "hiA", "hiB", "splitA", "splitB", "doneA", "doneB", "low_free",
            "high_free", "ff_hi", "ff_split", "h2_in", "sum_split", "sum_done", "sum_root", "eps_set",
            "xres0", "xres1", "x2_ready", "x2_hi", "x2_split", "p_in", "pp_turned", "pp_hi",
            "pp_split", "y_ready", "y_turned", "y_out", "y_stored", "ones_set", "gains_set",
            "pads_set")}

        DS = lambda i, n=1: bass.ds(i, n)
        block = top.enter_context(nc.Block())

        @block.sync
        def _(sp):
            def const(dst, src):
                sp.dma_start(dst, src).then_inc(consts_in, 16)

            with nc.allow_non_contiguous_dma(reason="gain columns, loaded once"):
                const(ident[:], ident_d)
                const(rope_c[:], cos_d)
                const(rope_s[:], sin_d)
                const(edge[:], edge_d.partition_broadcast(P))
                const(gqk[:, 0, :], q_norm.partition_broadcast(P))
                const(gqk[:, 1, :], k_norm.partition_broadcast(P))
                const(gin[:], g_mix_pre.rearrange("(k p) -> p k", p=P))
                const(pscale[:], pool_scale.rearrange("(k p) -> p k", p=P))
                const(gpost2[:], g_ffn_post.rearrange("(k p) -> p k", p=P))
                const(bgate[:], b_pgate.rearrange("(k p) -> p k", p=P))
            sp.dma_start(raw[:, 0, 0:NPOOL * P].rearrange("p (g n) -> p g n", g=NPOOL),
                         pool_w.rearrange("g c d -> c g d")).then_inc(S["pw_raw"], 16)

            def strip(g, k):
                sp.wait_ge(S["strip_split"], g * 16 + k + 1)
                src = w_in[k * P:(k + 1) * P, :] if k < KT else w_out[(k - KT) * P:(k - KT + 1) * P, :]
                sp.dma_start(raw[:, k % 2, 0:src.shape[1]], src).then_inc(S[f"raw_in{k % 2}"], 16)

            sp.wait_ge(S["pw_split"], 1)
            with sp.Fori(0, NSEQ) as g:
                stages[sp] = (g, 0)
                for t in range(2):
                    sp.dma_start(xs_a[:, t, :], x[DS(g * NT + t), :, :].rearrange("t p d -> p (t d)"))\
                        .then_inc(S[f"xa_in{t}"], 16)
                for k in range(KT):
                    strip(g, k)
                with sp.Fori(0, NT // 2 - 1) as i:
                    for j in range(2):
                        t = 2 * i + 2 + j
                        sp.wait_ge(S["h_ready"], g * NT + t - 1)
                        sp.dma_start(xs_a[:, j, :], x[DS(g * NT + t), :, :].rearrange("t p d -> p (t d)"))\
                            .then_inc(S[f"xa_in{j}"], 16)
                stage_end(sp)
                for k in range(KT, KT + 6):
                    strip(g, k)
                stage_end(sp)
                sp.dma_start(gpost[:], g_mix_post.partition_broadcast(P)).then_inc(S["gains_in"], 16)
                sp.dma_start(gffn[:], g_ffn_pre.partition_broadcast(P)).then_inc(S["gains_in"], 16)
                for t in range(2):
                    sp.dma_start(xs_d[:, t, :], x[DS(g * NT + t), :, :].rearrange("t p d -> p (t d)"))\
                        .then_inc(S[f"xd_in{t}"], 16)
                for k in range(KT + 6, 2 * KT):
                    strip(g, k)

                def store(t, c, o):
                    n = g * NT + t
                    sp.wait_ge(S["x1_out"], n + 1)
                    sp.dma_start(x1t_d[DS(c), :, :, o:o + P].rearrange("c p k n -> p (c k) n"),
                                 x1t[:]).then_inc(S["x1_stored"], 16)
                    sp.wait_ge(S["h2_out"], n + 1)
                    for e in range(2):
                        sp.dma_start(h2t_d[e, DS(c), :, :, o:o + P].rearrange("c p k n -> p (c k) n"),
                                     h2t[:, e].bitcast(F32)).then_inc(S["h2_stored"], 16)

                for t in range(NT):
                    store(t, 2 * g + t // 4, (t % 4) * P)
                    if t + 2 < NT:
                        sp.wait_ge(S["x1_ready"], g * NT + t + 1)
                        sp.dma_start(xs_d[:, t % 2, :], x[DS(g * NT + t + 2), :, :].rearrange("t p d -> p (t d)"))\
                            .then_inc(S[f"xd_in{t % 2}"], 16)
                sp.wait_ge(S["x1_stored"], (g + 1) * NT * 16)
                alone(sp)
                sp.wait_ge(S["h2_stored"], (g + 1) * NT * 32)
                alone(sp)
                stage_end(sp)

            def load(b, side, src_a):
                sp.wait_ge(S["split" + "AB"[side]], b)
                kts, cols = src_a.shape[1], src_a.shape[2]
                sp.dma_start(rawb[:, side, 0:kts * cols].rearrange("p (k n) -> p k n", k=kts), src_a)\
                    .then_inc(S["raw" + "AB"[side]], 16)

            def cols(w, k0, kts, at, n):
                return w[k0 * P:(k0 + kts) * P, DS(at, n)].rearrange("(k p) n -> p k n", p=P)

            def gate_up(b, part):
                with sp.Fori(0, GU[part]) as i:
                    at = i * 256 + PART0[part] * P
                    load(b + i, 0, cols(w_gate, 0, KT, at, 256))
                    load(b + i, 1, cols(w_up, 0, KT, at, 256))

            def down(b, part):
                half = PARTS[part] // 2
                with sp.Fori(0, DN) as i:
                    load(b + i, 0, cols(w_down, PART0[part], half, i * 512, 512))
                    load(b + i, 1, cols(w_down, PART0[part] + half, half, i * 512, 512))

            def ple(b):
                with sp.Fori(0, NPLE) as i:
                    load(b + i, 0, cols(w_pgate, 0, KT, i * 256, 256))
                    load(b + i, 1, cols(w_proj, 0, PLE // P, i * 256, 256))

            def chunk(b, with_ple):
                gate_up(b, 0)
                b = b + GU[0]
                if with_ple:
                    ple(b)
                    b = b + NPLE
                down(b, 0)
                b = b + DN
                for part in (1, 2):
                    gate_up(b, part)
                    down(b + GU[part], part)
                    b = b + GU[part] + DN

            chunk(0, False)
            with sp.Fori(0, NCH - 1) as c:
                chunk(BODIES0 + c * BODIES, True)
            ple(BODIES0 + (NCH - 1) * BODIES)

        @block.gpsimd
        def _(pool):
            step = Signal(S["step_g"])

            def go(ins):
                step.by(ins)
                pool.wait_ge(step.sem, step.value)
                alone(pool)

            nc.gpsimd.memset(chan[:], 0.0).then_inc(S["pads_set"], 1)
            with repeat(pool, NSEQ, {step: POOL_STEPS}) as g:
                stages[pool] = (g, 0)
                stage_end(pool)

                def windows(job):
                    grp, hf = job // 2, job % 2
                    u = chan[:, grp + 1, :]
                    t0 = hf * 512
                    w = WINDOWS[grp]
                    lo, hi = 8, 520
                    reach = []
                    for lev in range(grp, -1, -1):
                        reach.insert(0, (lo, hi))
                        d = 2 ** lev // 2 if lev else 0
                        lo, hi = lo - d, hi + d
                    for lev in range(grp + 1):
                        a, b = reach[lev]
                        out = win_s[:, lev % 2, a:b]
                        if lev == 0:
                            go(nc.gpsimd.tensor_tensor(out, u[:, t0 + a - 1:t0 + b - 1],
                                                       u[:, t0 + a:t0 + b], ALU.add))
                        else:
                            d = 2 ** lev // 2
                            prev = win_s[:, (lev - 1) % 2, :]
                            go(nc.gpsimd.tensor_tensor(out, prev[:, a - d:b - d], prev[:, a + d:b + d],
                                                       ALU.add))
                    s = win_s[:, grp % 2, :]
                    m = win_s[:, (grp + 1) % 2, :]
                    at = 8 if hf == 0 else 512
                    go(nc.gpsimd.tensor_tensor(s[:, at:at + PAD], s[:, at:at + PAD],
                                               edge[:, grp, hf, :], ALU.mult))
                    go(nc.gpsimd.tensor_scalar(s[:, 8:520], s[:, 8:520], 1.0 / w, None, ALU.mult))
                    go(nc.gpsimd.tensor_tensor(m[:, 8:520], s[:, 8:520],
                                               u[:, PAD + t0:PAD + t0 + 512], ALU.subtract))
                    if job >= 1:
                        pool.wait_ge(S["misc_done"], g * NMISC + MISC[("pool", job - 1)] + 1)
                        alone(pool)
                    go(nc.gpsimd.tensor_copy(mt_hl[:, 0, :], m[:, 8:520]))
                    nc.gpsimd.tensor_tensor(mt_hl[:, 1, :], m[:, 8:520], mt_hl[:, 0, :].bitcast(F32),
                                            ALU.subtract).then_inc(S["m_ready"], 1)

                def add_parts(hc):
                    h, half = hc // 2, hc % 2
                    pool.wait_ge(S["misc_free"], g * NMISC + MISC[("o", hc)] + 1)
                    nc.gpsimd.tensor_tensor(heads[:, 4 * half:4 * half + 4, h, :], oparts[:, 0],
                                            oparts[:, 1], ALU.add).then_inc(S["o_added"], 1)

                def q_split(h, half):
                    if h:
                        pool.wait_ge(S["misc_done"], g * NMISC + MISC[("q", h - 1, half)] + 1)
                        alone(pool)
                    rows = heads[:, 4 * half:4 * half + 4, h, :]
                    go(nc.gpsimd.tensor_copy(qh[:, half, :, 0, :].bitcast(F32R), rows))
                    nc.gpsimd.tensor_tensor(qh[:, half, :, 1, :], rows, qh[:, half, :, 0, :],
                                            ALU.subtract).then_inc(S["qh_ready"], 1)

                for half in range(2):
                    q_split(0, half)
                for h in range(NH):
                    for half in range(2):
                        if h + 1 < NH:
                            q_split(h + 1, half)
                    if h:
                        add_parts(2 * h - 2)
                    windows(h)
                    if h:
                        add_parts(2 * h - 1)
                add_parts(2 * NH - 2)
                add_parts(2 * NH - 1)
                stage_end(pool)
                with pool.Fori(0, NT // 2) as i:
                    for j in range(2):
                        n = g * NT + 2 * i + j
                        pool.wait_ge(S["mix_read"], n + 1)
                        pool.wait_ge(S[f"xd_in{j}"], (g * (NT // 2) + i + 1) * 16)
                        pool.wait_ge(S["h2_ready"], n)
                        pool.wait_ge(S["x1_turned"], n)
                        nc.gpsimd.tensor_tensor(x1[:], mixn[:], xs_d[:, j, :], ALU.add)\
                            .then_inc(S["x1_ready"], 1)
                stage_end(pool)

            def load_h2(c):
                for e in range(2):
                    pool.dma_start(h2c[:, e].bitcast(F32), h2t_d[e, DS(c)].rearrange("c p k n -> p (c k) n"))\
                        .then_inc(S["h2_in"], 16)

            def load_p(c):
                pool.wait_ge(S["pp_turned"], c)
                pool.dma_start(ptok[:], p[DS(c * 4, 4)].rearrange("t p n -> p t n")).then_inc(S["p_in"], 16)

            def load_xres(c):
                with pool.Fori(0, 2) as i:
                    for s in range(2):
                        pool.wait_ge(S["x2_ready"], c * 4 + 2 * i + s + 1)
                        pool.dma_start(xres[:, s], x1t_d[DS(c), :, DS(4 * i + 2 * s, 2), :]
                                       .rearrange("c p k n -> p (c k) n")).then_inc(S[f"xres{s}"], 16)

            def store_y(c):
                with pool.Fori(0, NPLE) as i:
                    pool.wait_ge(S["y_out"], c * NPLE + i + 1)
                    pool.dma_start(y[DS(c * 4, 4), :, DS(i * 256, 256)].rearrange("t p n -> p t n"),
                                   yrow[:]).then_inc(S["y_stored"], 16)

            def end_of_chunk(c):
                pool.wait_ge(S["doneB"], 2 * (BODIES0 + c * BODIES - DN))
                load_h2((c + 1) % NCH)

            def embedding(c):
                load_p(c)
                load_xres(c)
                store_y(c)

            load_h2(0)
            end_of_chunk(0)
            with pool.Fori(0, NCH - 1) as c:
                embedding(c)
                end_of_chunk(c + 1)
            embedding(NCH - 1)
            pool.wait_ge(S["y_stored"], 16 * NCH * NPLE)
            pool.wait_ge(S["h2_in"], 32 * (NCH + 1))

        def passes(w, xm):
            return ((w[0], xm[0]), (w[0], xm[1]), (w[1], xm[0]))

        @block.tensor
        def _(pe):
            def mm(out, lhs, rhs, start, stop):
                return nc.tensor.matmul(out, lhs, rhs, start=start, stop=stop)

            def turn(out, src):
                return nc.tensor.transpose(out, src, ident[:])

            pe.wait_ge(consts_in, 16 * NCONST)
            pe.sem_inc(S["q_done"], 2)
            with pe.Fori(0, NSEQ) as g:
                stages[pe] = (g, 0)

                def turn_x(t):
                    n = g * NT + t
                    pe.wait_ge(S["h_ready"], n + 1)
                    pe.wait_ge(S["ht_split"], n)
                    for k in range(KT):
                        last = turn(ps[:, k // 4, (k % 4) * P:(k % 4 + 1) * P], hrow[:, k * P:(k + 1) * P])
                    last.then_inc(S["x_turned"], 1)

                def columns(out, s, at, n, first_waits=None):
                    for k in range(KT):
                        if first_waits is not None:
                            pe.wait_ge(S["strip_split"], g * 16 + k + 3)
                        for m, (a, b) in enumerate(((0, 0), (0, 1), (1, 0))):
                            last = mm(out, ht[:, s, a, k, :], win[:, b, k, at:at + n],
                                      k == 0 and m == 0, k == KT - 1 and m == 2)
                    return last

                def project(t, s, ahead):
                    n = g * NT + t
                    pe.wait_ge(S["ht_split"], n + 1)
                    pe.wait_ge(S["v_split"], n)
                    columns(ps[:, 4, 0:2 * KV_W], s, POOL_W + Q_W, 2 * KV_W, g).then_inc(S["kv_done"], 1)
                    pe.wait_ge(S["u_out"], n)
                    columns(ps[:, 2, :], s, 0, POOL_W).then_inc(S["u_done"], 1)
                    if ahead:
                        turn_x(t + 1)
                    pe.wait_ge(S["q_out"], n)
                    columns(ps[:, 3, :], s, POOL_W, Q_W).then_inc(S["q_done"], 1)
                    pe.wait_ge(S["u_out"], n + 1)
                    pe.wait_ge(S["u_stored"], n)
                    for k in range(NPOOL):
                        last = turn(ps[:, 5, k * P:(k + 1) * P], utok[:, k * P:(k + 1) * P])
                    last.then_inc(S["u_turned"], 1)
                    pe.wait_ge(S["k_stack"], n + 1)
                    pe.wait_ge(S["k_stored"], n)
                    for k in range(4):
                        last = turn(ps[:, 6, k * P:(k + 1) * P],
                                    kstack[:, k // 2, 2 * (k % 2):2 * (k % 2) + 2, :]
                                    .rearrange("p a d -> p (a d)"))
                    last.then_inc(S["k_turned"], 1)

                turn_x(0)
                with pe.Fori(0, NT // 2 - 1) as i:
                    project(2 * i, 0, True)
                    project(2 * i + 1, 1, True)
                project(NT - 2, 0, True)
                project(NT - 1, 1, False)
                stage_end(pe)

                def misc(key):
                    pe.wait_ge(S["misc_free"], g * NMISC + MISC[key])

                def turn_q(h, half):
                    misc(("q", h, half))
                    pe.wait_ge(S["qh_ready"], (g * NH + h) * 2 + half + 1)
                    for t in range(4):
                        last = turn(ps[:, 7, t * P:(t + 1) * P], qh[:, half, t].rearrange("p a d -> p (a d)"))
                    last.then_inc(S["misc_done"], 1)

                def scores(s):
                    h, u = s // NT, s % NT
                    if s >= 2:
                        pe.wait_ge(S["exp_done"], g * NSTEP + s - 1)
                    if u == 0:
                        pe.wait_ge(S["misc_free"], g * NMISC + MISC[("q", h, 1)] + 1)
                    b = 2 * (s % 2)
                    for a in range(2):
                        for c in range(2):
                            last = mm(ps[:, b + c, :], qs[:, h % 2, u * P:(u + 1) * P],
                                      keys[:, h // GROUP, a, c * 512:(c + 1) * 512], a == 0, a == 1)
                    last.then_inc(S["score_done"], 1)

                def turn_p(s, half):
                    pe.wait_ge(S["exp_done"], g * NSTEP + s + 1)
                    if s >= 1:
                        pe.wait_ge(S["p_split"], 2 * (g * NSTEP + s - 1) + half + 1)
                    for k in range(4):
                        kt = 4 * half + k
                        last = turn(ps[:, 4 + half, k * P:(k + 1) * P],
                                    prob[:, s % 2, kt * P:(kt + 1) * P])
                    last.then_inc(S["p_turned"], 1)

                def pv(hc, j):
                    h, b = hc // 2, hc % 2
                    pe.wait_ge(S["p_split"], 2 * (g * NSTEP + 4 * hc + 3) + j // 2 + 1)
                    if j == 0 and hc >= 1:
                        pe.wait_ge(S["o_out"], g * 2 * NH + hc)
                    for kt in (2 * j, 2 * j + 1):
                        for e in range(2):
                            last = mm(ps[:, 6, :], values[:, kt, h // GROUP].rearrange("p a d -> p (a d)"),
                                      pt[:, b, e, kt, :], kt == 0 and e == 0, kt == KT - 1 and e == 1)
                    if j == 3:
                        last.then_inc(S["pv_done"], 1)

                def turn_o(hc):
                    misc(("o", hc))
                    pe.wait_ge(S["o_out"], g * 2 * NH + hc + 1)
                    for t in range(4):
                        last = turn(ps[:, 7, t * P:(t + 1) * P], ot[:, t * P:(t + 1) * P])
                    last.then_inc(S["misc_done"], 1)

                def pooled(job):
                    misc(("pool", job))
                    pe.wait_ge(S["m_ready"], g * NH + job + 1)
                    for m, (a, b) in enumerate(((0, 0), (0, 1), (1, 0))):
                        last = mm(ps[:, 7, :], poolw[:, a, job // 2, :], mt_hl[:, b, :], m == 0, m == 2)
                    last.then_inc(S["misc_done"], 1)

                turn_q(0, 0)
                turn_q(0, 1)
                scores(0)
                scores(1)
                for s in range(NSTEP):
                    h, u = s // NT, s % NT
                    if s + 2 < NSTEP:
                        scores(s + 2)
                    turn_p(s, 0)
                    if s >= 4:
                        pv(s // 4 - 1, s % 4)
                    turn_p(s, 1)
                    if u in (0, 4) and h:
                        turn_o(2 * h - 2 + u // 4)
                    if u in (1, 3) and h + 1 < NH:
                        turn_q(h + 1, u // 2)
                    if u == 7:
                        pooled(h)
                turn_o(2 * NH - 2)
                for j in range(4):
                    pv(2 * NH - 1, j)
                turn_o(2 * NH - 1)
                stage_end(pe)

                def turn_a(t):
                    n = g * NT + t
                    pe.wait_ge(S["c_split"], n)
                    rows = heads[:, t].rearrange("p h d -> p (h d)")
                    for k in range(4):
                        last = turn(ps[:, 0, k * P:(k + 1) * P], rows[:, k * P:(k + 1) * P])
                    last.then_inc(S["a_turned"], 1)

                def mix_half(t, s, c, first):
                    n = g * NT + t
                    if c == 0:
                        pe.wait_ge(S["c_split"], n + 1)
                        if not first:
                            pe.wait_ge(S["mix_read"], n - 1)
                    for k in range(KT):
                        if first:
                            pe.wait_ge(S["strip_split"], g * 16 + KT + k + 3)
                        wo, kk = (wout_a, k) if k < KT // 2 else (wout_b, k - KT // 2)
                        for m, (a, b) in enumerate(((0, 0), (0, 1), (1, 0))):
                            last = mm(ps[:, 1 + 2 * s + c, :], ct[:, s, a, k, :],
                                      wo[:, b, kk, c * 512:(c + 1) * 512],
                                      k == 0 and m == 0, k == KT - 1 and m == 2)
                    last.then_inc(S["mix_done"], 1)

                def turn_back(t, which):
                    n = g * NT + t
                    if which == 0:
                        pe.wait_ge(S["x1_ready"], n + 1)
                        pe.wait_ge(S["h2_out"], n)
                    else:
                        pe.wait_ge(S["h2_ready"], n + 1)
                        pe.wait_ge(S["x1_out"], n + 1)
                    src = (x1, h2)[which]
                    for k in range(KT):
                        last = turn(ps[:, 5 + k // 4, (k % 4) * P:(k % 4 + 1) * P], src[:, k * P:(k + 1) * P])
                    last.then_inc(S[("x1_turned", "h2_turned")[which]], 1)

                turn_a(0)
                for t in range(NT):
                    mix_half(t, t % 2, 0, t == 0)
                    if t + 1 < NT:
                        turn_a(t + 1)
                    if t:
                        turn_back(t - 1, 0)
                    mix_half(t, t % 2, 1, False)
                    if t:
                        turn_back(t - 1, 1)
                turn_back(NT - 1, 0)
                turn_back(NT - 1, 1)
                stage_end(pe)

            def side(b, sd):
                pe.wait_ge(S["split" + "AB"[sd]], b + 1)
                pe.wait_ge(S[("low_free", "high_free")[sd]], 2 * b)

            def gate_up(b, times):
                with pe.Fori(0, times) as i:
                    for sd in range(2):
                        side(b + i, sd)
                        w = wb[:, sd].rearrange("p e (k n) -> p e k n", k=KT)
                        for j in range(2):
                            for k in range(KT):
                                for m, (a, e) in enumerate(((0, 0), (0, 1), (1, 0))):
                                    last = mm(ps[:, 2 * sd + j, :], w[:, a, k, j * P:(j + 1) * P],
                                              h2c[:, e, k, :], k == 0 and m == 0, k == KT - 1 and m == 2)
                            last.then_inc(S["done" + "AB"[sd]], 1)

            def down(b, part, tiles, between=None):
                half = PARTS[part] // 2
                for i in range(DN):
                    for sd in range(2):
                        if sd == 0:
                            side(b + i, 0)
                        else:
                            pe.wait_ge(S["splitB"], b + i + 1)
                        w = wb[:, sd, :, 0:half * 512].rearrange("p e (k n) -> p e k n", k=half)
                        for j in range(4):
                            if sd == 0 and j == 2:
                                pe.wait_ge(S["high_free"], 2 * (b + i))
                            for k in range(half):
                                if i == 0 and j == 0:
                                    pe.wait_ge(S["ff_split"], tiles + sd * half + k + 1)
                                for m, (a, e) in enumerate(((0, 0), (0, 1), (1, 0))):
                                    last = mm(ps[:, j, :], w[:, a, k, j * P:(j + 1) * P],
                                              ff[:, e, sd * half + k, :],
                                              sd == 0 and k == 0 and m == 0,
                                              sd == 1 and k == half - 1 and m == 2)
                            if j % 2:
                                last.then_inc(S["done" + "AB"[sd]], 1)
                    if i == 0 and between:
                        between()

            def token_sums(c):
                pe.wait_ge(S["sum_split"], c + 1)
                for e in range(2):
                    last = mm(ps[:, 6, :], ones[:], sumhl[:, e, :], e == 0, e == 1)
                last.then_inc(S["sum_done"], 1)
                pe.wait_ge(S["p_in"], 16 * (c + 1))
                pe.wait_ge(S["y_out"], c * NPLE)
                for k in range(2):
                    for t in range(4):
                        last = turn(ps[:, 4 + k, t * P:(t + 1) * P], ptok[:, t, k * P:(k + 1) * P])
                last.then_inc(S["pp_turned"], 1)

            def turn_y(c, i):
                pe.wait_ge(S["y_ready"], c * NPLE + i + 1)
                pe.wait_ge(S["y_out"], c * NPLE + i)
                pe.wait_ge(S["pp_split"], c + 1)
                for t in range(4):
                    for j in range(2):
                        last = turn(ps[:, 4 + t // 2, ((t % 2) * 2 + j) * P:((t % 2) * 2 + j + 1) * P],
                                    ft[:, 2 * i + j, t * P:(t + 1) * P])
                last.then_inc(S["y_turned"], 1)

            def ple(b, c):
                for i in range(NPLE):
                    for sd in range(2):
                        side(b + i, sd)
                        if i == 0 and sd == 1:
                            pe.wait_ge(S["pp_split"], c + 1)
                        kts = (KT, PLE // P)[sd]
                        w = wb[:, sd, :, 0:kts * 256].rearrange("p e (k n) -> p e k n", k=kts)
                        act = (x2, pturn)[sd]
                        for j in range(2):
                            for k in range(kts):
                                if i == 0 and sd == 0 and j == 0:
                                    pe.wait_ge(S["x2_split"], c * (KT // 2) + k // 2 + 1)
                                for m, (a, e) in enumerate(((0, 0), (0, 1), (1, 0))):
                                    last = mm(ps[:, 2 * sd + j, :], w[:, a, k, j * P:(j + 1) * P],
                                              act[:, e, k, :], k == 0 and m == 0, k == kts - 1 and m == 2)
                            last.then_inc(S["done" + "AB"[sd]], 1)
                    if i:
                        turn_y(c, i - 1)

            def chunk(b, c, before):
                pe.wait_ge(S["h2_in"], 32 * (c + 1))
                alone(pe)
                gate_up(b, 1)
                if before is not None:
                    token_sums(before)
                gate_up(b + 1, GU[0] - 1)
                b = b + GU[0]
                if before is not None:
                    ple(b, before)
                    b = b + NPLE
                down(b, 0, c * 22, (lambda: turn_y(before, NPLE - 1)) if before is not None else None)
                b = b + DN
                for part in (1, 2):
                    gate_up(b, GU[part])
                    down(b + GU[part], part, c * 22 + PART0[part])
                    b = b + GU[part] + DN

            pe.wait_ge(S["ones_set"], 1)
            chunk(0, 0, None)
            with pe.Fori(0, NCH - 1) as c:
                chunk(BODIES0 + c * BODIES, c + 1, c)
            token_sums(NCH - 1)
            ple(BODIES0 + (NCH - 1) * BODIES, NCH - 1)
            turn_y(NCH - 1, NPLE - 1)

        @block.scalar
        def _(act):
            copy = lambda out, src, **k: nc.scalar.activation(out, src, ACT.Copy, **k)

            def root(out, sums, n):
                return nc.scalar.activation(out, sums, ACT.Sqrt, bias=eps[:, 0:1], scale=1.0 / n)

            act.wait_ge(consts_in, 16 * NCONST)
            act.wait_ge(S["eps_set"], 1)
            act.wait_ge(S["pw_raw"], 16)
            copy(poolw[:, 0], raw[:, 0, 0:NPOOL * P].rearrange("p (g n) -> p g n", g=NPOOL))\
                .then_inc(S["pw_hi"], 1)

            with act.Fori(0, NSEQ) as g:
                stages[act] = (g, 0)

                def strip(k):
                    act.wait_ge(S[f"raw_in{k % 2}"], (g * 8 + k // 2 + 1) * 16)
                    if k < KT:
                        ins = copy(win[:, 0, k, :], raw[:, k % 2, :], scale=gin[:, k:k + 1])
                    elif k < KT + 4:
                        ins = copy(wout_a[:, 0, k - KT, :], raw[:, k % 2, 0:D])
                    else:
                        ins = copy(wout_b[:, 0, k - KT - 4, :], raw[:, k % 2, 0:D])
                    ins.then_inc(S["strip_hi"], 1)

                def square(i, s):
                    act.wait_ge(S[f"xa_in{s}"], (g * (NT // 2) + i + 1) * 16)
                    nc.scalar.activation(junk_a[:], xs_a[:, s, :], ACT.Square,
                                         accum_out=small[:, s:s + 1]).then_inc(S["x_sum"], 1)
                    act.wait_ge(S["x_sum"], g * NT + 2 * i + s + 1)
                    root(small[:, s:s + 1], small[:, s:s + 1], D).then_inc(S["x_root"], 1)

                def turned_hi(n, s):
                    act.wait_ge(S["x_turned"], n + 1)
                    act.wait_ge(S["q_done"], n + 1)
                    copy(ht[:, s, 0].rearrange("p k n -> p (k n)"), pair(0)).then_inc(S["ht_hi"], 1)

                def project(i, s, ahead):
                    t = 2 * i + s
                    n = g * NT + t
                    if ahead:
                        square(i + s, 1 - s)
                    act.wait_ge(S["kv_done"], n + 1)
                    copy(values[:, DS(t), :, 0, :].rearrange("p t k d -> p (t k) d"),
                         ps[:, 4, KV_W:2 * KV_W].rearrange("p (k d) -> p k d", k=NKV)).then_inc(S["v_hi"], 1)
                    act.wait_ge(S["k_stack"], n)
                    copy(ktok[:].rearrange("p k d -> p (k d)"), ps[:, 4, 0:KV_W]).then_inc(S["k_raw"], 1)
                    act.wait_ge(S["k_sums"], n + 1)
                    root(small[:, 6:6 + NKV], small[:, 6:6 + NKV], HD).then_inc(S["k_root"], 1)
                    act.wait_ge(S["u_done"], n + 1)
                    act.wait_ge(S["u_turned"], n)
                    copy(utok[:], ps[:, 2, :]).then_inc(S["u_out"], 1)
                    if ahead:
                        turned_hi(n + 1, 1 - s)
                    act.wait_ge(S["q_done"], n + 3)
                    act.wait_ge(S["q_rope"], n)
                    copy(qtok[:].rearrange("p h d -> p (h d)"), ps[:, 3, :]).then_inc(S["q_out"], 1)
                    act.wait_ge(S["q_sums"], n + 1)
                    nc.scalar.activation(small[:, 6:6 + NH], small[:, 6:6 + NH], ACT.Sqrt,
                                         bias=eps[:, 1:2], scale=1.0).then_inc(S["q_root"], 1)
                    act.wait_ge(S["u_turned"], n + 1)
                    copy(chan[:, 1:NPOOL + 1, DS(PAD + t * P, P)],
                         ps[:, 5, :].rearrange("p (g n) -> p g n", g=NPOOL)).then_inc(S["u_stored"], 1)
                    act.wait_ge(S["k_turned"], n + 1)
                    copy(keys[:, :, :, DS(t * P, P)].rearrange("p k a n -> p (k a) n"),
                         ps[:, 6, :].rearrange("p (g n) -> p g n", g=4)).then_inc(S["k_stored"], 1)

                act.wait_ge(S["pads_set"], 1)
                square(0, 0)
                turned_hi(g * NT, 0)
                for k in range(KT):
                    strip(k)
                with act.Fori(0, NT // 2 - 1) as i:
                    project(i, 0, True)
                    project(i, 1, True)
                project(NT // 2 - 1, 0, True)
                project(NT // 2 - 1, 1, False)
                stage_end(act)

                def exp(s):
                    act.wait_ge(S["max_done"], g * NSTEP + s + 1)
                    if s >= 2:
                        act.wait_ge(S["p_turned"], 2 * (g * NSTEP + s - 2) + 2)
                    nc.scalar.activation(prob[:, s % 2, :], pair(2 * (s % 2)), ACT.Exp,
                                         bias=negmax[:, s:s + 1], scale=1.0,
                                         accum_out=rowsum[:, s:s + 1]).then_inc(S["exp_done"], 1)

                def misc_wait(key):
                    act.wait_ge(S["misc_done"], g * NMISC + MISC[key] + 1)

                def q_out(h, half):
                    misc_wait(("q", h, half))
                    if half == 0 and h >= 2:
                        act.wait_ge(S["score_done"], g * NSTEP + NT * (h - 1))
                    copy(qs[:, h % 2, half * 512:(half + 1) * 512], ps[:, 7, :]).then_inc(S["misc_free"], 1)

                def o_out(hc):
                    act.wait_ge(S["pv_done"], g * 2 * NH + hc + 1)
                    if hc >= 1:
                        act.wait_ge(S["misc_done"], g * NMISC + MISC[("o", hc - 1)] + 1)
                    copy(ot[:], ps[:, 6, :]).then_inc(S["o_out"], 1)

                q_out(0, 0)
                q_out(0, 1)
                exp(0)
                exp(1)
                for s in range(NSTEP):
                    h, u = s // NT, s % NT
                    for half in range(2):
                        act.wait_ge(S["p_turned"], 2 * (g * NSTEP + s) + half + 1)
                        if half == 0 and u % 4 == 0 and s >= 8:
                            act.wait_ge(S["pv_done"], g * 2 * NH + s // 4 - 1)
                        copy(pt[:, (s // 4) % 2, 0, 4 * half:4 * half + 4, (u % 4) * P:(u % 4 + 1) * P],
                             ps[:, 4 + half, :].rearrange("p (k n) -> p k n", k=4)).then_inc(S["p_hi"], 1)
                        if half == 0 and s % 4 == 3 and s >= 7:
                            o_out(s // 4 - 1)
                    if s + 2 < NSTEP:
                        exp(s + 2)
                    if u in (1, 3) and h + 1 < NH:
                        q_out(h + 1, u // 2)
                    if u == 7:
                        misc_wait(("pool", h))
                        t0 = PAD + (h % 2) * 512
                        copy(chan[:, h // 2, t0:t0 + 512], ps[:, 7, :],
                             scale=pscale[:, h // 2:h // 2 + 1]).then_inc(S["misc_free"], 1)
                    if s % 8 == 2 and s // 8 < 4:
                        strip(KT + s // 8)
                o_out(2 * NH - 1)
                stage_end(act)

                def concat_hi(t, s):
                    n = g * NT + t
                    if t >= 2:
                        act.wait_ge(S["mix_done"], 2 * (n - 1))
                    copy(ct[:, s, 0, 0:4, :], chan[:, 0:NPOOL, PAD + t * P:PAD + (t + 1) * P])
                    act.wait_ge(S["a_turned"], n + 1)
                    copy(ct[:, s, 0, 4:8, :], ps[:, 0, :].rearrange("p (k n) -> p k n", k=4))\
                        .then_inc(S["c_hi"], 1)

                def post_a(t):
                    n = g * NT + t
                    act.wait_ge(S["mix_done"], 2 * (n + 1))
                    nc.scalar.activation(junk_d[:], pair(1 + 2 * (t % 2)), ACT.Square,
                                         accum_out=small[:, 4:5]).then_inc(S["m_sum"], 1)
                    act.wait_ge(S["m_sum"], n + 1)
                    root(small[:, 4:5], small[:, 4:5], D).then_inc(S["m_root"], 1)

                def post_b(t):
                    n = g * NT + t
                    act.wait_ge(S["x1_ready"], n + 1)
                    nc.scalar.activation(junk_d[:], x1[:], ACT.Square,
                                         accum_out=small[:, 5:6]).then_inc(S["x1_sum"], 1)
                    act.wait_ge(S["x1_sum"], n + 1)
                    root(small[:, 5:6], small[:, 5:6], D).then_inc(S["x1_root"], 1)
                    act.wait_ge(S["x1_turned"], n + 1)
                    act.wait_ge(S["x1_stored"], n * 16)
                    copy(x1t[:].rearrange("p k n -> p (k n)"), pair(5)).then_inc(S["x1_out"], 1)
                    act.wait_ge(S["h2_turned"], n + 1)
                    act.wait_ge(S["h2_stored"], n * 32)
                    copy(h2t[:, 0].rearrange("p k n -> p (k n)"), pair(5)).then_inc(S["h2_hi"], 1)

                concat_hi(0, 0)
                for k in range(KT + 4, 2 * KT):
                    strip(k)
                for t in range(NT):
                    if t:
                        post_a(t - 1)
                    if t + 1 < NT:
                        concat_hi(t + 1, (t + 1) % 2)
                    if t:
                        post_b(t - 1)
                post_a(NT - 1)
                post_b(NT - 1)
                stage_end(act)

            def weights(b, sd, n):
                ab = "AB"[sd]
                act.wait_ge(S["raw" + ab], 16 * (b + 1))
                act.wait_ge(S["done" + ab], 2 * b)
                copy(wb[:, sd, 0, 0:n], rawb[:, sd, 0:n]).then_inc(S["hi" + ab], 1)

            def weights(b, sd):
                ab = "AB"[sd]
                act.wait_ge(S["raw" + ab], 16 * (b + 1))
                act.wait_ge(S["done" + ab], 2 * b)
                copy(wb[:, sd, 0], rawb[:, sd]).then_inc(S["hi" + ab], 1)

            def gate_up(b, tile, fn=ACT.Silu):
                for j in range(2):
                    act.wait_ge(S["doneA"], 2 * b + j + 1)
                    act.wait_ge(S["high_free"], 2 * b)
                    nc.scalar.activation(gated[:, j, :], ps[:, j, :], ACT.Silu).then_inc(S["low_free"], 1)
                weights(b + 1, 0)
                for j in range(2):
                    act.wait_ge(S["high_free"], 2 * b + j + 1)
                    copy(ff[:, 0, DS(tile + j), :].rearrange("p k n -> p (k n)"), prod[:, j, :])\
                        .then_inc(S["ff_hi"], 1)
                weights(b + 1, 1)

            def gate_ups(b, times, first=0):
                with act.Fori(0, times) as i:
                    gate_up(b + i, 2 * i + first)

            def y_rows(c, i):
                act.wait_ge(S["y_turned"], c * NPLE + i + 1)
                act.wait_ge(S["y_stored"], 16 * (c * NPLE + i))
                copy(yrow[:].rearrange("p t n -> p (t n)"), pair(4)).then_inc(S["y_out"], 1)

            def down(b, part, c=None):
                def body(b, i):
                    weights(b, 0)
                    if part == 0:
                        for q in range(2):
                            act.wait_ge(S["doneB"], 2 * (b - 1) + q + 1)
                            copy(ft[:, DS(4 * i + 2 * q, 2), :].rearrange("p k n -> p (k n)"), pair(2 * q))\
                                .then_inc(S[("low_free", "high_free")[q]], 2)
                    weights(b, 1)

                if c is None:
                    with act.Fori(0, DN) as i:
                        body(b + i + 1, i)
                else:
                    body(b + 1, 0)
                    y_rows(c, NPLE - 1)
                    body(b + 2, 1)

            def x2_pairs(c, i):
                for q in range(2):
                    n = 2 * i + q
                    act.wait_ge(S["x2_ready"], c * 4 + n + 3)
                    copy(x2[:, 0, DS(2 * n, 2), :].rearrange("p k n -> p (k n)"),
                         ft[:, DS(2 * n, 2), :].rearrange("p k n -> p (k n)")).then_inc(S["x2_hi"], 1)

            def embedded_rows(c):
                act.wait_ge(S["sum_done"], c + 1)
                root(rnorm[:], ps[:, 6, :], D).then_inc(S["sum_root"], 1)
                act.wait_ge(S["pp_turned"], c + 1)
                copy(pturn[:, 0].rearrange("p k n -> p (k n)"), pair(4)).then_inc(S["pp_hi"], 1)

            def ple_body(b, c, i, last=False):
                if not last:
                    weights(b + 1, 0)
                for j in range(2):
                    act.wait_ge(S["doneA"], 2 * b + j + 1)
                    act.wait_ge(S["high_free"], 2 * b)
                    nc.scalar.activation(gated[:, j, :], ps[:, j, :], ACT.Sigmoid,
                                         bias=bgate[:, DS(2 * i + j)]).then_inc(S["low_free"], 1)

            def ple(b, c, end=False):
                ple_body(b, c, 0)
                weights(b + 1, 1)
                with act.Fori(1, NPLE - 1) as i:
                    ple_body(b + i, c, i)
                    y_rows(c, i - 1)
                    weights(b + i + 1, 1)
                ple_body(b + NPLE - 1, c, NPLE - 1, end)
                y_rows(c, NPLE - 2)
                if not end:
                    weights(b + NPLE, 1)

            def chunk(b, before):
                if before is None:
                    gate_ups(b, GU[0])
                    b = b + GU[0]
                else:
                    gate_up(b, 0)
                    embedded_rows(before)
                    with act.Fori(0, 2) as i:
                        x2_pairs(before, i)
                        gate_up(b + i + 1, 2 * i + 2)
                    gate_up(b + 3, 6)
                    b = b + GU[0]
                    ple(b, before)
                    b = b + NPLE
                down(b, 0, before)
                b = b + DN
                for part in (1, 2):
                    gate_ups(b, GU[part])
                    down(b + GU[part], part)
                    b = b + GU[part] + DN

            weights(0, 0)
            weights(0, 1)
            chunk(0, None)
            with act.Fori(0, NCH - 1) as c:
                chunk(BODIES0 + c * BODIES, c)
            embedded_rows(NCH - 1)
            with act.Fori(0, 2) as i:
                x2_pairs(NCH - 1, i)
            ple(BODIES0 + (NCH - 1) * BODIES, NCH - 1, True)
            y_rows(NCH - 1, NPLE - 1)

        @block.vector
        def _(dve):
            step = Signal(S["step_v"])
            V = nc.vector

            def go(ins):
                step.by(ins)
                dve.wait_ge(step.sem, step.value)

            f = lambda ap: ap.bitcast(F32)

            dve.wait_ge(consts_in, 16 * NCONST)
            V.memset(ones[:].bitcast(F32), 1.0).then_inc(S["ones_set"], 1)
            V.memset(eps[:, 0:1], EPS)
            V.memset(eps[:, 1:2], HD * EPS).then_inc(S["eps_set"], 1)
            dve.wait_ge(S["pw_hi"], 1)
            V.tensor_tensor(poolw[:, 1], raw[:, 0, 0:NPOOL * P].rearrange("p (g n) -> p g n", g=NPOOL),
                            f(poolw[:, 0]), ALU.subtract).then_inc(S["pw_split"], 1)
            dve.sem_inc(S["strip_split"], 2)

            def head_sums(src, h, done):
                a = tmp_a[:, 0:h, :]
                go(V.tensor_tensor(a, src, src, ALU.mult))
                V.tensor_reduce(small[:, 6:6 + h], a, AX.X, ALU.add).then_inc(done, 1)

            def head_norm_rope(src, h, gain, t, out, rooted, n):
                a, b, r = tmp_a[:, 0:h, :], tmp_b[:, 0:h, :], small[:, 6:6 + h]
                dve.wait_ge(rooted, n + 1)
                go(V.reciprocal(r, r))
                go(V.tensor_tensor(src, src, r.unsqueeze(2).to_broadcast([P, h, HD]), ALU.mult))
                go(V.tensor_tensor(src, src, gqk[:, gain:gain + 1, :].to_broadcast([P, h, HD]), ALU.mult))
                two = lambda ap: ap.rearrange("p h (d e) -> p h d e", e=2)
                row = lambda tb: tb[:, DS(t), :].unsqueeze(3).to_broadcast([P, h, HD // 2, 2])
                V.tensor_tensor(two(a), two(src), row(rope_c), ALU.mult)
                go(V.tensor_tensor(two(b), two(src), row(rope_s), ALU.mult))
                V.tensor_tensor(two(out)[:, :, :, 0], two(a)[:, :, :, 0], two(b)[:, :, :, 1], ALU.subtract)
                return V.tensor_tensor(two(out)[:, :, :, 1], two(b)[:, :, :, 0], two(a)[:, :, :, 1], ALU.add)

            with repeat(dve, NSEQ, {step: V_STEPS}) as g:
                stages[dve] = (g, 0)

                def strip(k):
                    dve.wait_ge(S["strip_hi"], g * 16 + k + 1)
                    if k < KT:
                        V.scalar_tensor_tensor(out=win[:, 1, k, :], in0=raw[:, k % 2, :],
                                               scalar=gin[:, k:k + 1], in1=f(win[:, 0, k, :]),
                                               op0=ALU.mult, op1=ALU.subtract).then_inc(S["strip_split"], 1)
                        return
                    w, kk = (wout_a, k - KT) if k < KT + 4 else (wout_b, k - KT - 4)
                    V.tensor_tensor(w[:, 1, kk, :], raw[:, k % 2, 0:D], f(w[:, 0, kk, :]),
                                    ALU.subtract).then_inc(S["strip_split"], 1)

                def norm(n, s):
                    dve.wait_ge(S["x_root"], n + 1)
                    go(V.reciprocal(small[:, 2:3], small[:, s:s + 1]))
                    dve.wait_ge(S["x_turned"], n)
                    V.tensor_scalar(hrow[:], xs_a[:, s, :], small[:, 2:3], None, ALU.mult)\
                        .then_inc(S["h_ready"], 1)

                def turned_lo(n, s):
                    dve.wait_ge(S["ht_hi"], n + 1)
                    V.tensor_tensor(ht[:, s, 1].rearrange("p k n -> p (k n)"), pair(0),
                                    f(ht[:, s, 0]).rearrange("p k n -> p (k n)"), ALU.subtract)\
                        .then_inc(S["ht_split"], 1)

                def project(i, s, ahead):
                    t = 2 * i + s
                    n = g * NT + t
                    dve.wait_ge(S["k_raw"], n + 1)
                    V.tensor_tensor(values[:, DS(t), :, 1, :].rearrange("p t k d -> p (t k) d"),
                                    ps[:, 4, KV_W:2 * KV_W].rearrange("p (k d) -> p k d", k=NKV),
                                    f(values[:, DS(t), :, 0, :]).rearrange("p t k d -> p (t k) d"),
                                    ALU.subtract).then_inc(S["v_split"], 1)
                    dve.wait_ge(S["q_rope"], n)
                    head_sums(ktok[:], NKV, S["k_sums"])
                    if ahead:
                        norm(n + 1, 1 - s)
                    go(head_norm_rope(ktok[:], NKV, 1, t, ktok[:], S["k_root"], n))
                    dve.wait_ge(S["k_turned"], n)
                    wide = ktok[:].unsqueeze(2).to_broadcast([P, NKV, 2, HD])
                    go(V.tensor_copy(kstack[:, :, 0:2, :].bitcast(F32R), wide))
                    V.tensor_tensor(kstack[:, :, 2:4, :], wide, kstack[:, :, 0:2, :], ALU.subtract)\
                        .then_inc(S["k_stack"], 1)
                    if ahead:
                        turned_lo(n + 1, 1 - s)
                    dve.wait_ge(S["q_out"], n + 1)
                    head_sums(qtok[:], NH, S["q_sums"])
                    head_norm_rope(qtok[:], NH, 0, t, heads[:, DS(t)].rearrange("p t h d -> p (t h) d"),
                                   S["q_root"], n)\
                        .then_inc(S["q_rope"], 1)

                norm(g * NT, 0)
                turned_lo(g * NT, 0)
                for k in range(KT):
                    strip(k)
                with repeat(dve, NT // 2 - 1, {step: 2 * AB_STEPS}) as i:
                    project(i, 0, True)
                    project(i, 1, True)
                project(NT // 2 - 1, 0, True)
                project(NT // 2 - 1, 1, False)
                stage_end(dve)

                def row_max(s):
                    dve.wait_ge(S["score_done"], g * NSTEP + s + 1)
                    V.tensor_reduce(negmax[:, s:s + 1], pair(2 * (s % 2)), AX.X, ALU.max, negate=True)\
                        .then_inc(S["max_done"], 1)

                def o_parts(hc):
                    dve.wait_ge(S["o_added"], g * 2 * NH + hc)
                    dve.wait_ge(S["exp_done"], g * NSTEP + 4 * hc + 4)
                    go(V.reciprocal(recip[:], rowsum[:, 4 * hc:4 * hc + 4]))
                    dve.wait_ge(S["misc_done"], g * NMISC + MISC[("o", hc)] + 1)
                    for e in range(2):
                        last = V.tensor_tensor(
                            oparts[:, e], ps[:, 7, :].rearrange("p (t e d) -> p t e d", t=4, e=2)[:, :, e, :],
                            recip[:].unsqueeze(2).to_broadcast([P, 4, HD]), ALU.mult)
                    last.then_inc(S["misc_free"], 1)

                row_max(0)
                row_max(1)
                for s in range(NSTEP):
                    h, u = s // NT, s % NT
                    if s + 2 < NSTEP:
                        row_max(s + 2)
                    for half in range(2):
                        dve.wait_ge(S["p_hi"], 2 * (g * NSTEP + s) + half + 1)
                        at = (slice(None), (s // 4) % 2, slice(None), slice(4 * half, 4 * half + 4),
                              slice((u % 4) * P, (u % 4 + 1) * P))
                        V.tensor_tensor(pt[at][:, 1], ps[:, 4 + half, :].rearrange("p (k n) -> p k n", k=4),
                                        f(pt[at][:, 0]), ALU.subtract).then_inc(S["p_split"], 1)
                    if u in (0, 4) and h:
                        o_parts(2 * h - 2 + u // 4)
                    if s % 8 == 2 and s // 8 < 4:
                        strip(KT + s // 8)
                o_parts(2 * NH - 2)
                o_parts(2 * NH - 1)
                stage_end(dve)

                def concat_lo(t, s):
                    dve.wait_ge(S["c_hi"], g * NT + t + 1)
                    V.tensor_tensor(ct[:, s, 1, 0:4, :], chan[:, 0:NPOOL, PAD + t * P:PAD + (t + 1) * P],
                                    f(ct[:, s, 0, 0:4, :]), ALU.subtract)
                    V.tensor_tensor(ct[:, s, 1, 4:8, :], ps[:, 0, :].rearrange("p (k n) -> p k n", k=4),
                                    f(ct[:, s, 0, 4:8, :]), ALU.subtract).then_inc(S["c_split"], 1)

                def post_a(t):
                    n = g * NT + t
                    dve.wait_ge(S["m_root"], n + 1)
                    go(V.reciprocal(small[:, 6:7], small[:, 4:5]))
                    dve.wait_ge(S["x1_ready"], n)
                    V.scalar_tensor_tensor(out=mixn[:], in0=pair(1 + 2 * (t % 2)), scalar=small[:, 6:7],
                                           in1=gpost[:], op0=ALU.mult, op1=ALU.mult)\
                        .then_inc(S["mix_read"], 1)

                def post_b(t):
                    n = g * NT + t
                    dve.wait_ge(S["x1_root"], n + 1)
                    go(V.reciprocal(small[:, 7:8], small[:, 5:6]))
                    dve.wait_ge(S["h2_turned"], n)
                    V.scalar_tensor_tensor(out=h2[:], in0=x1[:], scalar=small[:, 7:8], in1=gffn[:],
                                           op0=ALU.mult, op1=ALU.mult).then_inc(S["h2_ready"], 1)
                    dve.wait_ge(S["h2_hi"], n + 1)
                    V.tensor_tensor(h2t[:, 1].rearrange("p k n -> p (k n)"), pair(5),
                                    f(h2t[:, 0]).rearrange("p k n -> p (k n)"), ALU.subtract)\
                        .then_inc(S["h2_out"], 1)

                dve.wait_ge(S["gains_in"], 32 * (g + 1))
                concat_lo(0, 0)
                for k in range(KT + 4, 2 * KT):
                    strip(k)
                for t in range(NT):
                    if t:
                        post_a(t - 1)
                    if t + 1 < NT:
                        concat_lo(t + 1, (t + 1) % 2)
                    if t:
                        post_b(t - 1)
                post_a(NT - 1)
                post_b(NT - 1)
                stage_end(dve)

            def weights(b, sd):
                ab = "AB"[sd]
                dve.wait_ge(S["hi" + ab], b + 1)
                V.tensor_tensor(wb[:, sd, 1], rawb[:, sd], f(wb[:, sd, 0]), ALU.subtract)\
                    .then_inc(S["split" + ab], 1)

            def gate_up(b, tile, tiles):
                weights(b + 1, 0)
                for j in range(2):
                    dve.wait_ge(S["low_free"], 2 * b + j + 1)
                    dve.wait_ge(S["doneB"], 2 * b + j + 1)
                    V.tensor_tensor(prod[:, j, :], gated[:, j, :], ps[:, 2 + j, :], ALU.mult)\
                        .then_inc(S["high_free"], 1)
                    dve.wait_ge(S["ff_hi"], tiles + j + 1)
                    V.tensor_tensor(ff[:, 1, DS(tile + j), :].rearrange("p k n -> p (k n)"), prod[:, j, :],
                                    f(ff[:, 0, DS(tile + j), :]).rearrange("p k n -> p (k n)"),
                                    ALU.subtract).then_inc(S["ff_split"], 1)
                weights(b + 1, 1)

            def gate_ups(b, times, tiles):
                with dve.Fori(0, times) as i:
                    gate_up(b + i, 2 * i, tiles + 2 * i)

            def down(b, part, c=None):
                last = part == len(PARTS) - 1
                if last:
                    go(V.memset(sumsq[:], 0.0))
                    alone(dve)
                with repeat(dve, DN, {step: 6} if last else {}) as i:
                    weights(b + i + 1, 0)
                    if part:
                        for q in range(2):
                            dve.wait_ge(S["doneB"], 2 * (b + i) + q + 1)
                            rows = ft[:, DS(4 * i + 2 * q, 2), :]
                            done = S[("low_free", "high_free")[q]]
                            V.tensor_tensor(rows.rearrange("p k n -> p (k n)"),
                                            rows.rearrange("p k n -> p (k n)"), pair(2 * q), ALU.add)\
                                .then_inc(done, 2)
                            if last:
                                dve.wait_ge(done, 2 * (b + i) + 2)
                                go(V.tensor_tensor(sqs[:], rows, rows, ALU.mult))
                                for j in range(2):
                                    go(V.tensor_tensor(sumsq[:], sumsq[:], sqs[:, j], ALU.add))
                    weights(b + i + 1, 1)
                if last:
                    go(V.tensor_copy(sumhl[:, 0, :], sumsq[:]))
                    V.tensor_tensor(sumhl[:, 1, :], sumsq[:], f(sumhl[:, 0, :]), ALU.subtract)\
                        .then_inc(S["sum_split"], 1)

            def token_sums(c):
                dve.wait_ge(S["sum_root"], c + 1)
                go(V.reciprocal(rnorm[:], rnorm[:]))
                dve.wait_ge(S["pp_hi"], c + 1)
                V.tensor_tensor(pturn[:, 1].rearrange("p k n -> p (k n)"), pair(4),
                                f(pturn[:, 0]).rearrange("p k n -> p (k n)"), ALU.subtract)\
                    .then_inc(S["pp_split"], 1)

            def x2_pairs(c, i):
                for q in range(2):
                    n = 2 * i + q
                    if q:
                        dve.wait_ge(S["x2_ready"], c * 4 + n + 2)
                    for j in range(2):
                        last = V.scalar_tensor_tensor(
                            out=sqs[:, j, :], in0=ft[:, DS(2 * n + j), :].rearrange("p k n -> p (k n)"),
                            scalar=gpost2[:, DS(2 * n + j)], in1=rnorm[:], op0=ALU.mult, op1=ALU.mult)
                    go(last)
                    dve.wait_ge(S[f"xres{q}"], 16 * (c * 2 + i + 1))
                    V.tensor_tensor(ft[:, DS(2 * n, 2), :], sqs[:], xres[:, q], ALU.add)\
                        .then_inc(S["x2_ready"], 1)
                for q in range(2):
                    n = 2 * i + q
                    dve.wait_ge(S["x2_hi"], c * 4 + n + 1)
                    V.tensor_tensor(x2[:, 1, DS(2 * n, 2), :], ft[:, DS(2 * n, 2), :],
                                    f(x2[:, 0, DS(2 * n, 2), :]), ALU.subtract).then_inc(S["x2_split"], 1)

            def ple(b, c, end=False):
                def body(b, i, last):
                    if not last:
                        weights(b + 1, 0)
                    for j in range(2):
                        dve.wait_ge(S["low_free"], 2 * b + j + 1)
                        dve.wait_ge(S["doneB"], 2 * b + j + 1)
                        V.tensor_tensor(prod[:, j, :], gated[:, j, :], ps[:, 2 + j, :], ALU.mult)\
                            .then_inc(S["high_free"], 1)
                    dve.wait_ge(S["high_free"], 2 * b + 2)
                    rows = ft[:, DS(2 * i, 2), :]
                    V.tensor_tensor(rows, rows, prod[:], ALU.add).then_inc(S["y_ready"], 1)
                    if not last:
                        weights(b + 1, 1)

                with dve.Fori(0, NPLE - 1) as i:
                    body(b + i, i, False)
                body(b + NPLE - 1, NPLE - 1, end)

            def chunk(b, before, tiles):
                if before is None:
                    gate_ups(b, GU[0], tiles)
                    b = b + GU[0]
                else:
                    gate_up(b, 0, tiles)
                    token_sums(before)
                    with repeat(dve, 2, {step: 2}) as i:
                        x2_pairs(before, i)
                        gate_up(b + i + 1, 2 * i + 2, tiles + 2 * i + 2)
                    gate_up(b + 3, 6, tiles + 6)
                    b = b + GU[0]
                    ple(b, before)
                    b = b + NPLE
                down(b, 0)
                b = b + DN
                for part in (1, 2):
                    gate_ups(b, GU[part], tiles + PART0[part])
                    down(b + GU[part], part)
                    b = b + GU[part] + DN

            dve.sem_inc(S["x2_ready"], 2)
            weights(0, 0)
            weights(0, 1)
            chunk(0, None, 0)
            with repeat(dve, NCH - 1, {step: 19}) as c:
                chunk(BODIES0 + c * BODIES, c, (c + 1) * NHID)
            token_sums(NCH - 1)
            with repeat(dve, 2, {step: 2}) as i:
                x2_pairs(NCH - 1, i)
            ple(BODIES0 + (NCH - 1) * BODIES, NCH - 1, True)


def rope_tables():
    t = np.arange(SEQ)
    row, col = (t // GRID_W).astype(np.float32), (t % GRID_W).astype(np.float32)
    ax = HD // 2
    inv = (1.0 / (np.float32(ROPE_THETA) ** (np.arange(0, ax, 2, dtype=np.float32) / np.float32(ax))))
    inv = inv.astype(np.float32)
    ang = np.concatenate([row[:, None] * inv, col[:, None] * inv], axis=-1).astype(np.float32)
    lay = lambda a: np.ascontiguousarray(a.reshape(NT, P, HD // 2).transpose(1, 0, 2).astype(np.float32))
    return lay(np.cos(ang)), lay(np.sin(ang))


def edge_table():
    out = np.ones((NPOOL, 2, PAD), np.float32)
    for n, w in enumerate(WINDOWS):
        for side, t0 in enumerate((0, SEQ - PAD)):
            t = np.arange(t0, t0 + PAD)
            held = np.clip(t + w - 1 - w // 2, 0, SEQ - 1) - np.clip(t - w // 2, 0, SEQ - 1) + 1
            out[n, side] = w / held
    return out


def kernel(x_prompt, x_sample, p_prompt, p_sample, ln_mix_pre, ln_mix_post, w_in, pool_w, pool_scale,
           q_norm, k_norm, w_out, ln_ffn_pre, ln_ffn_post, w_gate, w_up, w_down,
           w_ple_proj, w_ple_gate, b_ple_gate):
    import concourse.bacc as bacc
    from concourse.bass_utils import run_bass_kernel_spmd

    nc = bacc.Bacc("TRN2", target_bir_lowering=False, num_devices=1)
    cos, sin = rope_tables()
    rows = lambda a, b, n: np.concatenate([np.asarray(a).reshape(NT, P, n), np.asarray(b).reshape(NT, P, n)])
    arrays = {
        "x": rows(x_prompt, x_sample, D), "p": rows(p_prompt, p_sample, PLE),
        "ident_d": np.eye(P, dtype=np.float32), "cos_d": cos, "sin_d": sin, "edge_d": edge_table(),
        "g_mix_pre": ln_mix_pre[0], "g_mix_post": ln_mix_post[0], "w_in": w_in[0], "pool_w": pool_w[0],
        "pool_scale": pool_scale[0], "q_norm": q_norm[0], "k_norm": k_norm[0], "w_out": w_out[0],
        "g_ffn_pre": ln_ffn_pre[0], "g_ffn_post": ln_ffn_post[0], "w_gate": w_gate[0], "w_up": w_up[0],
        "w_down": w_down[0], "w_proj": w_ple_proj[0], "w_pgate": w_ple_gate[0], "b_pgate": b_ple_gate[0],
    }
    arrays = {"in_" + k: np.ascontiguousarray(a) for k, a in arrays.items()}
    args = {k[3:]: nc.dram_tensor(k, a.shape, mybir.dt.from_np(a.dtype), kind="ExternalInput").ap()
            for k, a in arrays.items()}
    y = nc.dram_tensor("y", (NSEQ * NT, P, D), F32, kind="ExternalOutput").ap()
    encoder_layer(nc, **args, y=y)
    got = run_bass_kernel_spmd(nc, [arrays], core_ids=[0]).results[0]["y"]
    return tuple(got.reshape(NSEQ, 1, SEQ, D))
```

```python
from contextlib import ExitStack, contextmanager

import numpy as np

import concourse.bass as bass
from concourse import mybir

F32 = mybir.dt.float32
F32R = mybir.dt.float32r
BF16 = mybir.dt.bfloat16
ALU = mybir.AluOpType
ACT = mybir.ActivationFunctionType
AX = mybir.AxisListType

P = 128
D = 1024
SEQ = 1024
NSEQ = 2
KT = D // P
NT = SEQ // P
POOL_W = 512
NPOOL = 4
WINDOWS = (2, 4, 8, 16)
PAD = 8
HD = 64
NH = 8
NKV = 2
GROUP = NH // NKV
Q_W = NH * HD
KV_W = NKV * HD
IN_W = POOL_W + Q_W + 2 * KV_W
GRID_W = 64
ROPE_THETA = 10000.0
DFF = 2816
PLE = 256
EPS = 1e-6

CH = 512
NCH = NSEQ * SEQ // CH
PARTS = (8, 8, 6)
PART0 = (0, 8, 16)
NHID = DFF // P
GU = tuple(n // 2 for n in PARTS)
DN = 2
NPLE = KT // 2
BODIES0 = sum(GU) + 3 * DN
BODIES = BODIES0 + NPLE


class Signal:

    def __init__(self, sem, start=0):
        self.sem, self.base, self.count = sem, start, 0

    def by(self, ins, n=1):
        ins.then_inc(self.sem, n)
        self.count += n

    @property
    def value(self):
        return self.base + self.count


@contextmanager
def repeat(engine, times, steps):
    kept = {s: (s.base, s.count) for s in steps}
    with engine.Fori(0, times) as i:
        for s, k in steps.items():
            s.base, s.count = kept[s][0] + kept[s][1] + i * k, 0
        yield i
        for s, k in steps.items():
            assert s.count == k, (s.sem, s.count, k)
    for s, k in steps.items():
        s.base, s.count = kept[s][0], kept[s][1] + times * k


def misc_schedule():
    order = [("q", 0, 0), ("q", 0, 1)]
    for h in range(NH):
        if h:
            order.append(("o", 2 * h - 2))
        if h + 1 < NH:
            order += [("q", h + 1, 0), ("q", h + 1, 1)]
        if h:
            order.append(("o", 2 * h - 1))
        order.append(("pool", h))
    order += [("o", 2 * NH - 2), ("o", 2 * NH - 1)]
    return {k: n for n, k in enumerate(order)}


MISC = misc_schedule()
NMISC = len(MISC)
NSTEP = NH * NT
NCONST = 8
POOL_STEPS = 2 * sum(n + 5 for n in range(NPOOL)) + 2 * (NH - 1)
AB_STEPS = 13
V_STEPS = 138


def encoder_layer(nc, x, p, ident_d, cos_d, sin_d, edge_d, g_mix_pre, g_mix_post, w_in, pool_w,
                  pool_scale, q_norm, k_norm, w_out, g_ffn_pre, g_ffn_post, w_gate, w_up, w_down,
                  w_proj, w_pgate, b_pgate, y):
    x1t_d = nc.dram_tensor("x1_turned", (NCH, P, KT, CH), F32, kind="Internal").ap()
    h2t_d = nc.dram_tensor("h2_turned", (NCH, P, KT, CH), F32, kind="Internal").ap()

    top = ExitStack()
    with top:
        def sem(name):
            return top.enter_context(nc.semaphore(name))

        def sb(stack, name, shape, dt=F32):
            return stack.enter_context(nc.sbuf_tensor(name, shape, dt))

        ps = top.enter_context(nc.psum_tensor("ps", [P, 8, 512], F32))
        pair = lambda b: ps[:, b:b + 2, :].rearrange("p b n -> p (b n)")

        ident = sb(top, "ident", [P, P])
        ones = sb(top, "ones", [P, P], F32R)
        gpost2 = sb(top, "gpost2", [P, KT])
        bgate = sb(top, "bgate", [P, KT])
        small = sb(top, "small", [P, 16])
        eps = sb(top, "eps", [P, 2])

        consts_in = sem("consts_in")
        stage_done = sem("stage_done")
        stages = {}
        waited = {e: sem(f"waited_{n}") for n, e in enumerate(
            (nc.sync, nc.gpsimd, nc.tensor, nc.scalar, nc.vector))}

        def alone(e):
            e.sem_inc(waited[e], 1)

        def stage_end(e):
            g, n = stages[e]
            e.drain().then_inc(stage_done, 1)
            e.wait_ge(stage_done, 5 * (g * 3 + n + 1))
            alone(e)
            stages[e] = (g, n + 1)

        one = ExitStack()
        rope_c = sb(one, "rope_c", [P, NT, HD // 2])
        rope_s = sb(one, "rope_s", [P, NT, HD // 2])
        edge = sb(one, "edge", [P, NPOOL, 2, PAD])
        gqk = sb(one, "gqk", [P, 2, HD])
        gin = sb(one, "gin", [P, KT])
        pscale = sb(one, "pscale", [P, NPOOL])
        poolw = sb(one, "poolw", [P, 2, NPOOL, P], F32R)
        raw = sb(one, "raw", [P, 2, IN_W])
        heads = sb(one, "heads", [P, NT, NH, HD])
        s_k = ExitStack()
        keys = sb(s_k, "keys", [P, NKV, 2, SEQ], F32R)
        s_k.close()
        early = sb(one, "early", [P, 3, IN_W])
        sb(one, "early_rest", [P, 2 * NKV * SEQ - 3 * IN_W])
        values = sb(one, "values", [P, NT, NKV, 2, HD], F32R)
        chan = sb(one, "chan", [P, NPOOL + 1, SEQ + 2 * PAD])
        negmax = sb(one, "negmax", [P, NSTEP])
        rowsum = sb(one, "rowsum", [P, NSTEP])
        recip = sb(one, "recip", [P, 4])

        s_a = ExitStack()
        ht = sb(s_a, "ht", [P, 2, 2, KT, P], F32R)
        hrow = sb(s_a, "hrow", [P, D])
        junk_a = sb(s_a, "junk_a", [P, D], BF16)
        utok = sb(s_a, "utok", [P, POOL_W])
        qtok = sb(s_a, "qtok", [P, NH, HD])
        tmp_a = sb(s_a, "tmp_a", [P, NH, HD])
        tmp_b = sb(s_a, "tmp_b", [P, NH, HD])
        kstack = sb(s_a, "kstack", [P, NKV, 4, HD])
        xs_a = sb(s_a, "xs_a", [P, 2, D])
        win = sb(s_a, "win", [P, 2, KT, IN_W], F32R)
        ktok = sb(s_a, "ktok", [P, NKV, HD])
        s_a.close()

        s_w = ExitStack()
        wout_a = sb(s_w, "wout_a", [P, 2, KT // 2, D], F32R)
        s_c = ExitStack()
        pt = sb(s_c, "pt", [P, 2, 2, KT, 4 * P], F32R)
        prob = sb(s_c, "prob", [P, 2, SEQ])
        qh = sb(s_c, "qh", [P, 2, 4, 2, HD])
        qs = sb(s_c, "qs", [P, 2, SEQ], F32R)
        ot = sb(s_c, "ot", [P, 4 * P])
        oparts = sb(s_c, "oparts", [P, 2, 4, HD])
        win_s = sb(s_c, "win_s", [P, 2, 528])
        mt_hl = sb(s_c, "mt_hl", [P, 2, 512], F32R)
        s_c.close()
        s_d = ExitStack()
        xs_d = sb(s_d, "xs_d", [P, 2, D])
        wout_b = sb(s_d, "wout_b", [P, 2, KT // 2, D], F32R)
        ct = sb(s_d, "ct", [P, 2, 2, KT, P], F32R)
        x1t = sb(s_d, "x1t", [P, KT, P])
        h2t = sb(s_d, "h2t", [P, KT, P])
        mixn = sb(s_d, "mixn", [P, D])
        x1 = sb(s_d, "x1", [P, D])
        h2 = sb(s_d, "h2", [P, D])
        junk_d = sb(s_d, "junk_d", [P, D], BF16)
        gpost = sb(s_d, "gpost", [P, D])
        gffn = sb(s_d, "gffn", [P, D])
        s_d.close()
        s_w.close()
        one.close()

        two = ExitStack()
        h2c = sb(two, "h2c", [P, 2, KT, CH], F32R)
        ff = sb(two, "ff", [P, 2, max(PARTS), CH], F32R)
        raw_b = sb(two, "raw_b", [P, 8 * 256])
        x2 = sb(two, "x2", [P, 2, KT, CH], F32R)
        ft = sb(two, "ft", [P, KT, CH])
        wb = sb(two, "wb", [P, 2, 2, 8 * 256], F32R)
        ptok = sb(two, "ptok", [P, 4, PLE])
        pturn = sb(two, "pturn", [P, 2, 2, CH], F32R)
        yrow = sb(two, "yrow", [P, 4, 256])
        gated = sb(two, "gated", [P, 2, CH])
        prod = sb(two, "prod", [P, 2, CH])
        xres = sb(two, "xres", [P, 2, 2, CH])
        sumsq = sb(two, "sumsq", [P, CH])
        sumhl = sb(two, "sumhl", [P, 2, CH], F32R)
        rnorm = sb(two, "rnorm", [P, CH])
        sqs = sb(two, "sqs", [P, 2, CH])
        rawb = (sb(two, "raw_a", [P, 8 * 256]), raw_b)
        two.close()

        S = {n: sem(n) for n in (
            "first_in", "raw_in0", "raw_in1", "strip_in2", "strip_in3", "strip_in4", "strip_in5",
            "strip_in6", "strip_in7", "strip_hi", "strip_split", "xa_in0", "xa_in1", "x_sum", "x_root",
            "k_sums", "k_root", "q_sums", "q_root", "h_ready", "x_turned", "ht_hi", "ht_split", "kv_done",
            "u_done", "q_done", "v_hi", "k_raw", "v_split", "u_out", "q_out", "u_turned", "u_stored",
            "k_stack", "k_turned", "k_stored", "q_rope", "step_v", "step_g", "pw_raw", "pw_hi",
            "score_done", "max_done", "exp_done", "p_turned", "p_hi", "p_split", "pv_done", "o_out",
            "misc_done", "misc_free", "qh_ready", "o_added", "m_ready", "xd_in0", "xd_in1", "gains_in",
            "a_turned", "c_hi", "c_split", "mix_done", "m_sum", "m_root", "mix_read", "x1_ready", "x1_sum",
            "x1_root", "h2_ready", "x1_turned", "x1_out", "h2_turned", "h2_hi", "h2_out", "x1_stored",
            "h2_stored", "rawA", "rawB", "hiA", "hiB", "splitA", "splitB", "doneA", "doneB", "low_free",
            "high_free", "ff_hi", "ff_split", "h2_first0", "h2_first1", "h2_first2", "h2_first3", "h2_in0",
            "h2_in1", "h2_in2", "h2_in3", "h2_split", "squared", "memory_free", "sum_split", "sum_done",
            "sum_root", "eps_set", "xres0", "xres1", "x2_ready", "x2_hi", "x2_split", "p_in", "pp_turned",
            "pp_hi", "pp_split", "y_ready", "y_turned", "y_out", "y_stored", "ones_set", "pads_set")}

        DS = lambda i, n=1: bass.ds(i, n)

        def load_h2(e, c, landed="h2_in"):
            for j in range(4):
                e.dma_start(x2[:, 0, 2 * j:2 * j + 2].bitcast(F32),
                            h2t_d[DS(c), :, 2 * j:2 * j + 2, :].rearrange("c p k n -> p (c k) n"))\
                    .then_inc(S[f"{landed}{j}"], 16)

        def halves(side):
            return (slice(0, 1024), slice(1024, 2048)) if side == 0 else (slice(0, 2048),)

        def strip_place(k):
            if k < 2 or k >= KT:
                return raw[:, k % 2, 0:(IN_W if k < KT else D)], f"raw_in{k % 2}"
            if k < KT - 3:
                return early[:, k - 2, :], f"strip_in{k}"
            at = (k - KT + 3) * IN_W
            return heads[:].rearrange("p t h d -> p (t h d)")[:, at:at + IN_W], f"strip_in{k}"

        def strips_landed(g, k):
            if 2 <= k < KT:
                return (g + 1) * 16
            return (g * 5 + (0 if k < 2 else (k - KT) // 2 + 1) + 1) * 16
        block = top.enter_context(nc.Block())

        @block.sync
        def _(sp):
            def const(dst, src):
                sp.dma_start(dst, src).then_inc(consts_in, 16)

            def rows_in(n, slot):
                sp.dma_start(xs_a[:, slot, :], x[DS(n), :, :].rearrange("t p d -> p (t d)"))\
                    .then_inc(S[f"xa_in{slot}"], 16)

            def strip(k):
                src = w_in[k * P:(k + 1) * P, :] if k < KT else w_out[(k - KT) * P:(k - KT + 1) * P, :]
                dst, name = strip_place(k)
                sp.dma_start(dst, src).then_inc(S[name], 16)

            def load(b, side, src_a):
                if not (isinstance(b, int) and b == 0):
                    sp.wait_ge(S["split" + "AB"[side]], (2, 1)[side] * b)
                kts, cols = src_a.shape[1], src_a.shape[2]
                sp.dma_start(rawb[side][:, 0:kts * cols].rearrange("p (k n) -> p k n", k=kts), src_a)\
                    .then_inc(S["raw" + "AB"[side]], 16)

            def cols(w, k0, kts, at, n):
                return w[k0 * P:(k0 + kts) * P, DS(at, n)].rearrange("(k p) n -> p k n", p=P)

            rows_in(0, 0)
            sp.dma_start(ident[:], ident_d).then_inc(S["first_in"], 16)
            with nc.allow_non_contiguous_dma(reason="gain columns, loaded once"):
                sp.dma_start(gin[:], g_mix_pre.rearrange("(k p) -> p k", p=P)).then_inc(S["first_in"], 16)
                sp.dma_start(qtok[:].rearrange("p h d -> p (h d)").rearrange("p (g n) -> p g n", g=NPOOL),
                             pool_w.rearrange("g c d -> c g d")).then_inc(S["pw_raw"], 16)
                for k in range(KT - 3):
                    strip(k)
                rows_in(1, 1)
                const(rope_c[:], cos_d)
                const(rope_s[:], sin_d)
                const(edge[:], edge_d.partition_broadcast(P))
                const(gqk[:, 0, :], q_norm.partition_broadcast(P))
                const(gqk[:, 1, :], k_norm.partition_broadcast(P))
                const(pscale[:], pool_scale.rearrange("(k p) -> p k", p=P))
                const(gpost2[:], g_ffn_post.rearrange("(k p) -> p k", p=P))
                const(bgate[:], b_pgate.rearrange("(k p) -> p k", p=P))

            with sp.Fori(0, NSEQ) as g:
                stages[sp] = (g, 0)
                for k in range(KT - 3, KT):
                    strip(k)
                with sp.Fori(0, NT // 2 - 1) as i:
                    for j in range(2):
                        t = 2 * i + 2 + j
                        sp.wait_ge(S["h_ready"], g * NT + t - 1)
                        rows_in(g * NT + t, j)
                stage_end(sp)
                for k in range(KT, KT + 6):
                    sp.wait_ge(S["strip_split"], g * 16 + (k - KT if k < KT + 2 else k - 2) + 1)
                    strip(k)
                stage_end(sp)
                for k in range(KT + 6, 2 * KT):
                    sp.wait_ge(S["strip_split"], g * 16 + k - 1)
                    strip(k)
                for t in range(2):
                    sp.dma_start(xs_d[:, t, :], x[DS(g * NT + t), :, :].rearrange("t p d -> p (t d)"))\
                        .then_inc(S[f"xd_in{t}"], 16)
                load(0, 0, cols(w_gate, 0, KT, 0, 256))
                for k in range(2, KT - 3):
                    strip(k)
                for k in range(2):
                    sp.wait_ge(S["strip_split"], g * 16 + 2 * KT - 1 + k)
                    strip(k)

                def store(t, c, o):
                    n = g * NT + t
                    sp.wait_ge(S["x1_out"], n + 1)
                    sp.dma_start(x1t_d[DS(c), :, :, o:o + P].rearrange("c p k n -> p (c k) n"),
                                 x1t[:]).then_inc(S["x1_stored"], 16)
                    sp.wait_ge(S["h2_out"], n + 1)
                    sp.dma_start(h2t_d[DS(c), :, :, o:o + P].rearrange("c p k n -> p (c k) n"),
                                 h2t[:]).then_inc(S["h2_stored"], 16)

                for t in range(NT):
                    sp.wait_ge(S["x1_ready"], g * NT + t + 1)
                    if t + 2 < NT:
                        sp.dma_start(xs_d[:, t % 2, :],
                                     x[DS(g * NT + t + 2), :, :].rearrange("t p d -> p (t d)"))\
                            .then_inc(S[f"xd_in{t % 2}"], 16)
                    else:
                        rows_in((g * NT + NT + t % 2) % (NSEQ * NT), t % 2)
                    store(t, 2 * g + t // 4, (t % 4) * P)
                sp.wait_ge(S["rawA"], (g + 1) * 16)
                alone(sp)
                for k in range(KT - 3):
                    sp.wait_ge(S[strip_place(k)[1]], (g + 1) * (5 if k < 2 else 1) * 16 + 16)
                    alone(sp)
                stage_end(sp)

            def gate_up(b, part, first=0):
                with sp.Fori(first, GU[part]) as i:
                    at = i * 256 + PART0[part] * P
                    load(b + i, 0, cols(w_gate, 0, KT, at, 256))
                    load(b + i, 1, cols(w_up, 0, KT, at, 256))

            def down(b, part):
                half = PARTS[part] // 2
                with sp.Fori(0, DN) as i:
                    load(b + i, 0, cols(w_down, PART0[part], half, i * 512, 512))
                    load(b + i, 1, cols(w_down, PART0[part] + half, half, i * 512, 512))

            def ple(b):
                with sp.Fori(0, NPLE) as i:
                    load(b + i, 0, cols(w_pgate, 0, KT, i * 256, 256))
                    load(b + i, 1, cols(w_proj, 0, PLE // P, i * 256, 256))

            def chunk(b, with_ple):
                if with_ple:
                    gate_up(b, 0)
                else:
                    sp.wait_ge(S["h2_stored"], CH // P * 16)
                    load_h2(sp, 0, "h2_first")
                    load(0, 1, cols(w_up, 0, KT, 0, 256))
                    gate_up(b, 0, 1)
                b = b + GU[0]
                if with_ple:
                    ple(b)
                    b = b + NPLE
                down(b, 0)
                b = b + DN
                for part in (1, 2):
                    gate_up(b, part)
                    down(b + GU[part], part)
                    b = b + GU[part] + DN

            chunk(0, False)
            with sp.Fori(0, NCH - 1) as c:
                chunk(BODIES0 + c * BODIES, True)
            ple(BODIES0 + (NCH - 1) * BODIES)

        @block.gpsimd
        def _(pool):
            step = Signal(S["step_g"])

            def go(ins):
                step.by(ins)
                pool.wait_ge(step.sem, step.value)
                alone(pool)

            nc.gpsimd.memset(chan[:], 0.0).then_inc(S["pads_set"], 1)
            with repeat(pool, NSEQ, {step: POOL_STEPS}) as g:
                stages[pool] = (g, 0)
                stage_end(pool)

                def windows(job):
                    grp, hf = job // 2, job % 2
                    u = chan[:, grp + 1, :]
                    t0 = hf * 512
                    w = WINDOWS[grp]
                    lo, hi = 8, 520
                    reach = []
                    for lev in range(grp, -1, -1):
                        reach.insert(0, (lo, hi))
                        d = 2 ** lev // 2 if lev else 0
                        lo, hi = lo - d, hi + d
                    for lev in range(grp + 1):
                        a, b = reach[lev]
                        out = win_s[:, lev % 2, a:b]
                        if lev == 0:
                            go(nc.gpsimd.tensor_tensor(out, u[:, t0 + a - 1:t0 + b - 1],
                                                       u[:, t0 + a:t0 + b], ALU.add))
                        else:
                            d = 2 ** lev // 2
                            prev = win_s[:, (lev - 1) % 2, :]
                            go(nc.gpsimd.tensor_tensor(out, prev[:, a - d:b - d], prev[:, a + d:b + d],
                                                       ALU.add))
                    s = win_s[:, grp % 2, :]
                    m = win_s[:, (grp + 1) % 2, :]
                    at = 8 if hf == 0 else 512
                    go(nc.gpsimd.tensor_tensor(s[:, at:at + PAD], s[:, at:at + PAD],
                                               edge[:, grp, hf, :], ALU.mult))
                    go(nc.gpsimd.tensor_scalar(s[:, 8:520], s[:, 8:520], 1.0 / w, None, ALU.mult))
                    go(nc.gpsimd.tensor_tensor(m[:, 8:520], s[:, 8:520],
                                               u[:, PAD + t0:PAD + t0 + 512], ALU.subtract))
                    if job >= 1:
                        pool.wait_ge(S["misc_done"], g * NMISC + MISC[("pool", job - 1)] + 1)
                        alone(pool)
                    go(nc.gpsimd.tensor_copy(mt_hl[:, 0, :], m[:, 8:520]))
                    nc.gpsimd.tensor_tensor(mt_hl[:, 1, :], m[:, 8:520], mt_hl[:, 0, :].bitcast(F32),
                                            ALU.subtract).then_inc(S["m_ready"], 1)

                def add_parts(hc):
                    h, half = hc // 2, hc % 2
                    pool.wait_ge(S["misc_free"], g * NMISC + MISC[("o", hc)] + 1)
                    nc.gpsimd.tensor_tensor(heads[:, 4 * half:4 * half + 4, h, :], oparts[:, 0],
                                            oparts[:, 1], ALU.add).then_inc(S["o_added"], 1)

                def q_split(h, half):
                    pool.wait_ge(S["misc_done"],
                                 g * NMISC + MISC[("q", h - 1, half if h > 1 else 1)] + 1)
                    alone(pool)
                    rows = heads[:, 4 * half:4 * half + 4, h, :]
                    go(nc.gpsimd.tensor_copy(qh[:, half, :, 0, :].bitcast(F32R), rows))
                    nc.gpsimd.tensor_tensor(qh[:, half, :, 1, :], rows, qh[:, half, :, 0, :],
                                            ALU.subtract).then_inc(S["qh_ready"], 1)

                for h in range(NH):
                    for half in range(2):
                        if h + 1 < NH:
                            q_split(h + 1, half)
                    if h:
                        add_parts(2 * h - 2)
                    windows(h)
                    if h < 4:
                        pool.wait_ge(S["strip_hi"], g * 16 + KT + h + 1)
                        nc.gpsimd.tensor_tensor(wout_a[:, 1, h, :], strip_place(KT + h)[0],
                                                wout_a[:, 0, h, :].bitcast(F32), ALU.subtract)\
                            .then_inc(S["strip_split"], 1)
                    if h:
                        add_parts(2 * h - 1)
                add_parts(2 * NH - 2)
                add_parts(2 * NH - 1)
                stage_end(pool)
                pool.dma_start(gpost[:], g_mix_post.partition_broadcast(P)).then_inc(S["gains_in"], 16)
                pool.dma_start(gffn[:], g_ffn_pre.partition_broadcast(P)).then_inc(S["gains_in"], 16)
                stage_end(pool)

            def load_p(c):
                pool.wait_ge(S["pp_turned"], c)
                pool.dma_start(ptok[:], p[DS(c * 4, 4)].rearrange("t p n -> p t n")).then_inc(S["p_in"], 16)

            def load_xres(c):
                with pool.Fori(0, 2) as i:
                    for s in range(2):
                        pool.wait_ge(S["x2_ready"], c * 4 + 2 * i + s + 1)
                        pool.dma_start(xres[:, s], x1t_d[DS(c), :, DS(4 * i + 2 * s, 2), :]
                                       .rearrange("c p k n -> p (c k) n")).then_inc(S[f"xres{s}"], 16)

            def store_y(c):
                with pool.Fori(0, NPLE) as i:
                    pool.wait_ge(S["y_out"], c * NPLE + i + 1)
                    pool.dma_start(y[DS(c * 4, 4), :, DS(i * 256, 256)].rearrange("t p n -> p t n"),
                                   yrow[:]).then_inc(S["y_stored"], 16)

            def embedding(c):
                load_p(c)
                load_xres(c)
                store_y(c)

            pool.wait_ge(S["x1_stored"], NSEQ * NT * 16)
            pool.wait_ge(S["h2_stored"], NSEQ * NT * 16)
            for t in range(2):
                pool.wait_ge(S[f"xa_in{t}"], (NSEQ * (NT // 2) + 1) * 16)
            pool.sem_inc(S["memory_free"], 1)
            pool.wait_ge(S["h2_split"], 4)
            load_h2(pool, 1)
            with pool.Fori(0, NCH - 2) as c:
                embedding(c)
                pool.wait_ge(S["doneA"], 2 * (BODIES0 + c * BODIES + GU[0] + NPLE))
                pool.wait_ge(S["h2_split"], 4 * (c + 2))
                load_h2(pool, c + 2)
            embedding(NCH - 2)
            embedding(NCH - 1)
            pool.wait_ge(S["y_stored"], 16 * NCH * NPLE)

        def passes(w, xm):
            return ((w[0], xm[0]), (w[0], xm[1]), (w[1], xm[0]))

        @block.tensor
        def _(pe):
            def mm(out, lhs, rhs, start, stop):
                return nc.tensor.matmul(out, lhs, rhs, start=start, stop=stop)

            def turn(out, src):
                return nc.tensor.transpose(out, src, ident[:])

            pe.wait_ge(S["first_in"], 32)
            pe.sem_inc(S["q_done"], 2)
            g = 0

            def turn_x(t):
                n = g * NT + t
                pe.wait_ge(S["h_ready"], n + 1)
                pe.wait_ge(S["ht_split"], n)
                for k in range(KT):
                    last = turn(ps[:, k // 4, (k % 4) * P:(k % 4 + 1) * P], hrow[:, k * P:(k + 1) * P])
                last.then_inc(S["x_turned"], 1)

            turn_x(0)
            with pe.Fori(0, NSEQ) as g:
                stages[pe] = (g, 0)

                def columns(out, s, at, n):
                    for k in range(KT):
                        for m, (a, b) in enumerate(((0, 0), (0, 1), (1, 0))):
                            last = mm(out, ht[:, s, a, k, :], win[:, b, k, at:at + n],
                                      k == 0 and m == 0, k == KT - 1 and m == 2)
                    return last

                def first_columns():
                    for k in range(KT):
                        pe.wait_ge(S["strip_split"], g * 16 + k + 1)
                        for out, at, n in ((ps[:, 4, 0:2 * KV_W], POOL_W + Q_W, 2 * KV_W),
                                           (ps[:, 2, :], 0, POOL_W)):
                            for m, (a, b) in enumerate(((0, 0), (0, 1), (1, 0))):
                                last = mm(out, ht[:, 0, a, k, :], win[:, b, k, at:at + n],
                                          k == 0 and m == 0, k == KT - 1 and m == 2)
                            if k == KT - 1:
                                last.then_inc(S["u_done" if at == 0 else "kv_done"], 1)

                def project(t, s, ahead, first=False):
                    n = g * NT + t
                    pe.wait_ge(S["ht_split"], n + 1)
                    pe.wait_ge(S["v_split"], n)
                    if first:
                        pe.wait_ge(S["u_out"], n)
                        first_columns()
                    else:
                        columns(ps[:, 4, 0:2 * KV_W], s, POOL_W + Q_W, 2 * KV_W)\
                            .then_inc(S["kv_done"], 1)
                        pe.wait_ge(S["u_out"], n)
                        columns(ps[:, 2, :], s, 0, POOL_W).then_inc(S["u_done"], 1)
                    if ahead:
                        turn_x(t + 1)
                    pe.wait_ge(S["q_out"], n)
                    columns(ps[:, 3, :], s, POOL_W, Q_W).then_inc(S["q_done"], 1)
                    pe.wait_ge(S["u_out"], n + 1)
                    pe.wait_ge(S["u_stored"], n)
                    for k in range(NPOOL):
                        last = turn(ps[:, 5, k * P:(k + 1) * P], utok[:, k * P:(k + 1) * P])
                    last.then_inc(S["u_turned"], 1)
                    pe.wait_ge(S["k_stack"], n + 1)
                    pe.wait_ge(S["k_stored"], n)
                    for k in range(4):
                        last = turn(ps[:, 6, k * P:(k + 1) * P],
                                    kstack[:, k // 2, 2 * (k % 2):2 * (k % 2) + 2, :]
                                    .rearrange("p a d -> p (a d)"))
                    last.then_inc(S["k_turned"], 1)

                project(0, 0, True, first=True)
                project(1, 1, True)
                with pe.Fori(1, NT // 2 - 1) as i:
                    project(2 * i, 0, True)
                    project(2 * i + 1, 1, True)
                project(NT - 2, 0, True)
                project(NT - 1, 1, False)
                stage_end(pe)

                def misc(key):
                    pe.wait_ge(S["misc_free"], g * NMISC + MISC[key])

                def turn_q(h, half):
                    misc(("q", h, half))
                    pe.wait_ge(S["qh_ready"], (g * NH + h) * 2 + half + 1)
                    for t in range(4):
                        last = turn(ps[:, 7, t * P:(t + 1) * P], qh[:, half, t].rearrange("p a d -> p (a d)"))
                    last.then_inc(S["misc_done"], 1)

                def scores(s):
                    h, u = s // NT, s % NT
                    if s >= 2:
                        pe.wait_ge(S["exp_done"], g * NSTEP + s - 1)
                    if u % 4 == 0:
                        pe.wait_ge(S["misc_free"], g * NMISC + MISC[("q", h, u // 4)] + 1)
                    b = 2 * (s % 2)
                    for a in range(2):
                        for c in range(2):
                            last = mm(ps[:, b + c, :], qs[:, h % 2, u * P:(u + 1) * P],
                                      keys[:, h // GROUP, a, c * 512:(c + 1) * 512], a == 0, a == 1)
                    last.then_inc(S["score_done"], 1)

                def turn_p(s, half):
                    pe.wait_ge(S["exp_done"], g * NSTEP + s + 1)
                    if s >= 1:
                        pe.wait_ge(S["p_split"], 2 * (g * NSTEP + s - 1) + half + 1)
                    for k in range(4):
                        kt = 4 * half + k
                        last = turn(ps[:, 4 + half, k * P:(k + 1) * P],
                                    prob[:, s % 2, kt * P:(kt + 1) * P])
                    last.then_inc(S["p_turned"], 1)

                def pv(hc, j):
                    h, b = hc // 2, hc % 2
                    pe.wait_ge(S["p_split"], 2 * (g * NSTEP + 4 * hc + 3) + j // 2 + 1)
                    if j == 0 and hc >= 1:
                        pe.wait_ge(S["o_out"], g * 2 * NH + hc)
                    for kt in (2 * j, 2 * j + 1):
                        for e in range(2):
                            last = mm(ps[:, 6, :], values[:, kt, h // GROUP].rearrange("p a d -> p (a d)"),
                                      pt[:, b, e, kt, :], kt == 0 and e == 0, kt == KT - 1 and e == 1)
                    if j == 3:
                        last.then_inc(S["pv_done"], 1)

                def turn_o(hc):
                    misc(("o", hc))
                    pe.wait_ge(S["o_out"], g * 2 * NH + hc + 1)
                    for t in range(4):
                        last = turn(ps[:, 7, t * P:(t + 1) * P], ot[:, t * P:(t + 1) * P])
                    last.then_inc(S["misc_done"], 1)

                def pooled(job):
                    misc(("pool", job))
                    pe.wait_ge(S["m_ready"], g * NH + job + 1)
                    for m, (a, b) in enumerate(((0, 0), (0, 1), (1, 0))):
                        last = mm(ps[:, 7, :], poolw[:, a, job // 2, :], mt_hl[:, b, :], m == 0, m == 2)
                    last.then_inc(S["misc_done"], 1)

                turn_q(0, 0)
                turn_q(0, 1)
                scores(0)
                scores(1)
                for s in range(NSTEP):
                    h, u = s // NT, s % NT
                    if s + 2 < NSTEP:
                        scores(s + 2)
                    turn_p(s, 0)
                    if s >= 4:
                        pv(s // 4 - 1, s % 4)
                    turn_p(s, 1)
                    if u in (0, 4) and h:
                        turn_o(2 * h - 2 + u // 4)
                    if u in (1, 3) and h + 1 < NH:
                        turn_q(h + 1, u // 2)
                    if u == 7:
                        pooled(h)
                turn_o(2 * NH - 2)
                for j in range(4):
                    pv(2 * NH - 1, j)
                turn_o(2 * NH - 1)
                stage_end(pe)

                def turn_a(t):
                    n = g * NT + t
                    pe.wait_ge(S["c_split"], n)
                    rows = heads[:, t].rearrange("p h d -> p (h d)")
                    for k in range(4):
                        last = turn(ps[:, 0, k * P:(k + 1) * P], rows[:, k * P:(k + 1) * P])
                    last.then_inc(S["a_turned"], 1)

                def mix_strip(s, c, k):
                    wo, kk = (wout_a, k) if k < KT // 2 else (wout_b, k - KT // 2)
                    for m, (a, b) in enumerate(((0, 0), (0, 1), (1, 0))):
                        last = mm(ps[:, 1 + 2 * s + c, :], ct[:, s, a, k, :],
                                  wo[:, b, kk, c * 512:(c + 1) * 512],
                                  k == 0 and m == 0, k == KT - 1 and m == 2)
                    if k == KT - 1:
                        last.then_inc(S["mix_done"], 1)

                def mix_half(t, s, c):
                    n = g * NT + t
                    if c == 0:
                        pe.wait_ge(S["c_split"], n + 1)
                        pe.wait_ge(S["mix_read"], n - 1)
                    for k in range(KT):
                        mix_strip(s, c, k)

                def turn_back(t, which):
                    n = g * NT + t
                    if which == 0:
                        pe.wait_ge(S["x1_ready"], n + 1)
                        pe.wait_ge(S["h2_out"], n)
                    else:
                        pe.wait_ge(S["h2_ready"], n + 1)
                        pe.wait_ge(S["x1_out"], n + 1)
                    src = (x1, h2)[which]
                    for k in range(KT):
                        last = turn(ps[:, 5 + k // 4, (k % 4) * P:(k % 4 + 1) * P], src[:, k * P:(k + 1) * P])
                    last.then_inc(S[("x1_turned", "h2_turned")[which]], 1)

                turn_a(0)
                turn_a(1)
                pe.wait_ge(S["c_split"], g * NT + 1)
                for k in range(KT):
                    pe.wait_ge(S["strip_split"], g * 16 + KT + k + 1)
                    for c in range(2):
                        mix_strip(0, c, k)
                for t in range(1, NT):
                    mix_half(t, t % 2, 0)
                    if t + 1 < NT:
                        turn_a(t + 1)
                    if t >= 2:
                        turn_back(t - 2, 1)
                    mix_half(t, t % 2, 1)
                    turn_back(t - 1, 0)
                turn_back(NT - 2, 1)
                turn_back(NT - 1, 0)
                turn_x(NT)
                turn_back(NT - 1, 1)
                stage_end(pe)

            def side(b, sd):
                pe.wait_ge(S["split" + "AB"[sd]], (2 * b, b)[sd] + 1)
                pe.wait_ge(S[("low_free", "high_free")[sd]], 2 * b)

            def second_half(b, sd, j, k, width):
                if sd == 0 and j == 0 and k * width == 1024:
                    pe.wait_ge(S["splitA"], 2 * b + 2)

            def gate_up(b, times, rows=None):
                with pe.Fori(0, times) as i:
                    for sd in range(2):
                        side(b + i, sd)
                        w = wb[:, sd].rearrange("p e (k n) -> p e k n", k=KT)
                        for j in range(2):
                            for k in range(KT):
                                second_half(b + i, sd, j, k, 256)
                                if rows is not None and sd == 0 and j == 0:
                                    pe.wait_ge(S["h2_split"], 4 * rows + k // 2 + 1)
                                for m, (a, e) in enumerate(((0, 0), (0, 1), (1, 0))):
                                    last = mm(ps[:, 2 * sd + j, :], w[:, a, k, j * P:(j + 1) * P],
                                              h2c[:, e, k, :], k == 0 and m == 0, k == KT - 1 and m == 2)
                            last.then_inc(S["done" + "AB"[sd]], 1)

            def down(b, part, tiles, between=None):
                half = PARTS[part] // 2
                for i in range(DN):
                    for sd in range(2):
                        if sd == 0:
                            side(b + i, 0)
                        else:
                            pe.wait_ge(S["splitB"], b + i + 1)
                        w = wb[:, sd, :, 0:half * 512].rearrange("p e (k n) -> p e k n", k=half)
                        for j in range(4):
                            if sd == 0 and j == 2:
                                pe.wait_ge(S["high_free"], 2 * (b + i))
                            for k in range(half):
                                second_half(b + i, sd, j, k, 512)
                                if i == 0 and j == 0:
                                    pe.wait_ge(S["ff_split"], tiles + sd * half + k + 1)
                                for m, (a, e) in enumerate(((0, 0), (0, 1), (1, 0))):
                                    last = mm(ps[:, j, :], w[:, a, k, j * P:(j + 1) * P],
                                              ff[:, e, sd * half + k, :],
                                              sd == 0 and k == 0 and m == 0,
                                              sd == 1 and k == half - 1 and m == 2)
                            if j % 2:
                                last.then_inc(S["done" + "AB"[sd]], 1)
                    if i == 0 and between:
                        between()

            def token_sums(c):
                pe.wait_ge(S["sum_split"], c + 1)
                for e in range(2):
                    last = mm(ps[:, 6, :], ones[:], sumhl[:, e, :], e == 0, e == 1)
                last.then_inc(S["sum_done"], 1)
                pe.wait_ge(S["p_in"], 16 * (c + 1))
                pe.wait_ge(S["y_out"], c * NPLE)
                for k in range(2):
                    for t in range(4):
                        last = turn(ps[:, 4 + k, t * P:(t + 1) * P], ptok[:, t, k * P:(k + 1) * P])
                last.then_inc(S["pp_turned"], 1)

            def turn_y(c, i):
                pe.wait_ge(S["y_ready"], c * NPLE + i + 1)
                pe.wait_ge(S["y_out"], c * NPLE + i)
                pe.wait_ge(S["pp_split"], c + 1)
                for t in range(4):
                    for j in range(2):
                        last = turn(ps[:, 4 + t // 2, ((t % 2) * 2 + j) * P:((t % 2) * 2 + j + 1) * P],
                                    ft[:, 2 * i + j, t * P:(t + 1) * P])
                last.then_inc(S["y_turned"], 1)

            def ple(b, c):
                for i in range(NPLE):
                    for sd in range(2):
                        side(b + i, sd)
                        if i == 0 and sd == 1:
                            pe.wait_ge(S["pp_split"], c + 1)
                        kts = (KT, PLE // P)[sd]
                        w = wb[:, sd, :, 0:kts * 256].rearrange("p e (k n) -> p e k n", k=kts)
                        act = (x2, pturn)[sd]
                        for j in range(2):
                            for k in range(kts):
                                second_half(b + i, sd, j, k, 256)
                                if i == 0 and sd == 0 and j == 0:
                                    pe.wait_ge(S["x2_split"], c * (KT // 2) + k // 2 + 1)
                                for m, (a, e) in enumerate(((0, 0), (0, 1), (1, 0))):
                                    last = mm(ps[:, 2 * sd + j, :], w[:, a, k, j * P:(j + 1) * P],
                                              act[:, e, k, :], k == 0 and m == 0, k == kts - 1 and m == 2)
                            last.then_inc(S["done" + "AB"[sd]], 1)
                    if i:
                        turn_y(c, i - 1)

            def chunk(b, c, before):
                gate_up(b, 1, c)
                if before is not None:
                    token_sums(before)
                gate_up(b + 1, GU[0] - 1)
                b = b + GU[0]
                if before is not None:
                    ple(b, before)
                    b = b + NPLE
                down(b, 0, c * 22, (lambda: turn_y(before, NPLE - 1)) if before is not None else None)
                b = b + DN
                for part in (1, 2):
                    gate_up(b, GU[part])
                    down(b + GU[part], part, c * 22 + PART0[part])
                    b = b + GU[part] + DN

            pe.wait_ge(S["ones_set"], 1)
            chunk(0, 0, None)
            with pe.Fori(0, NCH - 1) as c:
                chunk(BODIES0 + c * BODIES, c + 1, c)
            token_sums(NCH - 1)
            ple(BODIES0 + (NCH - 1) * BODIES, NCH - 1)
            turn_y(NCH - 1, NPLE - 1)

        @block.scalar
        def _(act):
            copy = lambda out, src, **k: nc.scalar.activation(out, src, ACT.Copy, **k)

            def root(out, sums, n):
                return nc.scalar.activation(out, sums, ACT.Sqrt, bias=eps[:, 0:1], scale=1.0 / n)

            act.wait_ge(S["first_in"], 32)
            act.wait_ge(S["eps_set"], 1)
            act.wait_ge(S["pw_raw"], 16)
            copy(poolw[:, 0].rearrange("p g n -> p (g n)"), qtok[:].rearrange("p h d -> p (h d)"))\
                .then_inc(S["pw_hi"], 1)

            g = 0

            def square(i, s):
                act.wait_ge(S[f"xa_in{s}"], (g * (NT // 2) + i + 1) * 16)
                nc.scalar.activation(junk_a[:], xs_a[:, s, :], ACT.Square,
                                     accum_out=small[:, s:s + 1]).then_inc(S["x_sum"], 1)
                act.wait_ge(S["x_sum"], g * NT + 2 * i + s + 1)
                root(small[:, s:s + 1], small[:, s:s + 1], D).then_inc(S["x_root"], 1)

            def turned_hi(n, s):
                act.wait_ge(S["x_turned"], n + 1)
                act.wait_ge(S["q_done"], n + 1)
                copy(ht[:, s, 0].rearrange("p k n -> p (k n)"), pair(0)).then_inc(S["ht_hi"], 1)

            act.wait_ge(S["pads_set"], 1)
            square(0, 0)
            turned_hi(0, 0)
            with act.Fori(0, NSEQ) as g:
                stages[act] = (g, 0)

                def strip(k):
                    src, landed = strip_place(k)
                    act.wait_ge(S[landed], strips_landed(g, k))
                    if k < KT:
                        ins = copy(win[:, 0, k, :], src, scale=gin[:, k:k + 1])
                    elif k < KT + 4:
                        ins = copy(wout_a[:, 0, k - KT, :], src)
                    else:
                        ins = copy(wout_b[:, 0, k - KT - 4, :], src)
                    ins.then_inc(S["strip_hi"], 1)

                def project(i, s, ahead, rows=True):
                    t = 2 * i + s
                    n = g * NT + t
                    if rows:
                        square(i + 1, s)
                    act.wait_ge(S["kv_done"], n + 1)
                    copy(values[:, DS(t), :, 0, :].rearrange("p t k d -> p (t k) d"),
                         ps[:, 4, KV_W:2 * KV_W].rearrange("p (k d) -> p k d", k=NKV)).then_inc(S["v_hi"], 1)
                    act.wait_ge(S["k_stack"], n)
                    copy(ktok[:].rearrange("p k d -> p (k d)"), ps[:, 4, 0:KV_W]).then_inc(S["k_raw"], 1)
                    act.wait_ge(S["k_sums"], n + 1)
                    root(small[:, 6:6 + NKV], small[:, 6:6 + NKV], HD).then_inc(S["k_root"], 1)
                    act.wait_ge(S["u_done"], n + 1)
                    act.wait_ge(S["u_turned"], n)
                    copy(utok[:], ps[:, 2, :]).then_inc(S["u_out"], 1)
                    if ahead:
                        turned_hi(n + 1, 1 - s)
                    act.wait_ge(S["q_done"], n + 3)
                    act.wait_ge(S["q_rope"], n)
                    copy(qtok[:].rearrange("p h d -> p (h d)"), ps[:, 3, :]).then_inc(S["q_out"], 1)
                    act.wait_ge(S["q_sums"], n + 1)
                    nc.scalar.activation(small[:, 6:6 + NH], small[:, 6:6 + NH], ACT.Sqrt,
                                         bias=eps[:, 1:2], scale=1.0).then_inc(S["q_root"], 1)
                    act.wait_ge(S["u_turned"], n + 1)
                    copy(chan[:, 1:NPOOL + 1, DS(PAD + t * P, P)],
                         ps[:, 5, :].rearrange("p (g n) -> p g n", g=NPOOL)).then_inc(S["u_stored"], 1)
                    act.wait_ge(S["k_turned"], n + 1)
                    copy(keys[:, :, :, DS(t * P, P)].rearrange("p k a n -> p (k a) n"),
                         ps[:, 6, :].rearrange("p (g n) -> p g n", g=4)).then_inc(S["k_stored"], 1)

                for k in range(KT):
                    strip(k)
                    if k == 5:
                        square(0, 1)
                act.wait_ge(consts_in, 16 * NCONST)
                with act.Fori(0, NT // 2 - 1) as i:
                    project(i, 0, True)
                    project(i, 1, True)
                project(NT // 2 - 1, 0, True, rows=False)
                project(NT // 2 - 1, 1, False, rows=False)
                stage_end(act)

                def exp(s):
                    act.wait_ge(S["max_done"], g * NSTEP + s + 1)
                    if s >= 2:
                        act.wait_ge(S["p_turned"], 2 * (g * NSTEP + s - 2) + 2)
                    nc.scalar.activation(prob[:, s % 2, :], pair(2 * (s % 2)), ACT.Exp,
                                         bias=negmax[:, s:s + 1], scale=1.0,
                                         accum_out=rowsum[:, s:s + 1]).then_inc(S["exp_done"], 1)

                def misc_wait(key):
                    act.wait_ge(S["misc_done"], g * NMISC + MISC[key] + 1)

                def q_out(h, half):
                    misc_wait(("q", h, half))
                    if half == 0 and h >= 2:
                        act.wait_ge(S["score_done"], g * NSTEP + NT * (h - 1))
                    copy(qs[:, h % 2, half * 512:(half + 1) * 512], ps[:, 7, :]).then_inc(S["misc_free"], 1)

                def o_out(hc):
                    act.wait_ge(S["pv_done"], g * 2 * NH + hc + 1)
                    if hc >= 1:
                        act.wait_ge(S["misc_done"], g * NMISC + MISC[("o", hc - 1)] + 1)
                    copy(ot[:], ps[:, 6, :]).then_inc(S["o_out"], 1)

                q_out(0, 0)
                q_out(0, 1)
                exp(0)
                exp(1)
                for s in range(NSTEP):
                    h, u = s // NT, s % NT
                    for half in range(2):
                        act.wait_ge(S["p_turned"], 2 * (g * NSTEP + s) + half + 1)
                        if half == 0 and u % 4 == 0 and s >= 8:
                            act.wait_ge(S["pv_done"], g * 2 * NH + s // 4 - 1)
                        copy(pt[:, (s // 4) % 2, 0, 4 * half:4 * half + 4, (u % 4) * P:(u % 4 + 1) * P],
                             ps[:, 4 + half, :].rearrange("p (k n) -> p k n", k=4)).then_inc(S["p_hi"], 1)
                        if half == 0 and s % 4 == 3 and s >= 7:
                            o_out(s // 4 - 1)
                    if s + 2 < NSTEP:
                        exp(s + 2)
                    if u in (1, 3) and h + 1 < NH:
                        q_out(h + 1, u // 2)
                    if u == 7:
                        misc_wait(("pool", h))
                        t0 = PAD + (h % 2) * 512
                        copy(chan[:, h // 2, t0:t0 + 512], ps[:, 7, :],
                             scale=pscale[:, h // 2:h // 2 + 1]).then_inc(S["misc_free"], 1)
                    if s % 8 == 2 and s // 8 < 4:
                        strip(KT + s // 8)
                o_out(2 * NH - 1)
                stage_end(act)

                def concat_hi(t, s):
                    n = g * NT + t
                    if t >= 2:
                        act.wait_ge(S["mix_done"], 2 * (n - 1))
                    copy(ct[:, s, 0, 0:4, :], chan[:, 0:NPOOL, PAD + t * P:PAD + (t + 1) * P])
                    act.wait_ge(S["a_turned"], n + 1)
                    copy(ct[:, s, 0, 4:8, :], ps[:, 0, :].rearrange("p (k n) -> p k n", k=4))\
                        .then_inc(S["c_hi"], 1)

                def post_a(t):
                    n = g * NT + t
                    act.wait_ge(S["mix_done"], 2 * (n + 1))
                    nc.scalar.activation(junk_d[:], pair(1 + 2 * (t % 2)), ACT.Square,
                                         accum_out=small[:, 4:5]).then_inc(S["m_sum"], 1)
                    act.wait_ge(S["m_sum"], n + 1)
                    root(small[:, 4:5], small[:, 4:5], D).then_inc(S["m_root"], 1)

                def post_b(t):
                    n = g * NT + t
                    act.wait_ge(S["x1_ready"], n + 1)
                    nc.scalar.activation(junk_d[:], x1[:], ACT.Square,
                                         accum_out=small[:, 5:6]).then_inc(S["x1_sum"], 1)
                    act.wait_ge(S["x1_sum"], n + 1)
                    root(small[:, 5:6], small[:, 5:6], D).then_inc(S["x1_root"], 1)

                def x1_out(t):
                    n = g * NT + t
                    act.wait_ge(S["x1_turned"], n + 1)
                    act.wait_ge(S["x1_stored"], n * 16)
                    copy(x1t[:].rearrange("p k n -> p (k n)"), pair(5)).then_inc(S["x1_out"], 1)

                def h2_out(t):
                    n = g * NT + t
                    act.wait_ge(S["h2_turned"], n + 1)
                    act.wait_ge(S["h2_stored"], n * 16)
                    copy(h2t[:].rearrange("p k n -> p (k n)"), pair(5)).then_inc(S["h2_out"], 1)

                concat_hi(0, 0)
                for k in range(KT + 4, 2 * KT):
                    strip(k)
                for t in range(NT):
                    if t:
                        post_a(t - 1)
                    if t + 1 < NT:
                        concat_hi(t + 1, (t + 1) % 2)
                    if t >= 2:
                        h2_out(t - 2)
                    if t:
                        post_b(t - 1)
                        x1_out(t - 1)
                post_a(NT - 1)
                h2_out(NT - 2)
                square(NT // 2, 0)
                post_b(NT - 1)
                x1_out(NT - 1)
                turned_hi(g * NT + NT, 0)
                h2_out(NT - 1)
                stage_end(act)

            def weights(b, sd):
                ab = "AB"[sd]
                act.wait_ge(S["raw" + ab], 16 * (b + (2, 1)[sd]))
                act.wait_ge(S["done" + ab], 2 * b)
                for cut in halves(sd):
                    copy(wb[:, sd, 0, cut], rawb[sd][:, cut]).then_inc(S["hi" + ab], 1)

            def gate_up(b, tile):
                for j in range(2):
                    act.wait_ge(S["doneA"], 2 * b + j + 1)
                    act.wait_ge(S["high_free"], 2 * b)
                    nc.scalar.activation(gated[:, j, :], ps[:, j, :], ACT.Silu).then_inc(S["low_free"], 1)
                weights(b + 1, 0)
                for j in range(2):
                    act.wait_ge(S["high_free"], 2 * b + j + 1)
                    copy(ff[:, 0, DS(tile + j), :].rearrange("p k n -> p (k n)"), prod[:, j, :])\
                        .then_inc(S["ff_hi"], 1)
                weights(b + 1, 1)

            def gate_ups(b, times, first=0):
                with act.Fori(0, times) as i:
                    gate_up(b + i, 2 * i + first)

            def y_rows(c, i):
                act.wait_ge(S["y_turned"], c * NPLE + i + 1)
                act.wait_ge(S["y_stored"], 16 * (c * NPLE + i))
                copy(yrow[:].rearrange("p t n -> p (t n)"), pair(4)).then_inc(S["y_out"], 1)

            def split_h2(c, j):
                if isinstance(c, int) and c == 0:
                    act.wait_ge(S[f"h2_first{j}"], 16)
                else:
                    act.wait_ge(S[f"h2_in{j}"], 16 * c)
                copy(h2c[:, 0, 2 * j:2 * j + 2], x2[:, 0, 2 * j:2 * j + 2].bitcast(F32))\
                    .then_inc(S["h2_hi"], 1)

            def last_down(b, c, ahead):
                for i in range(DN):
                    weights(b + i + 1, 0)
                    if ahead:
                        act.wait_ge(S["doneB"], 2 * b)
                        for j in (2 * i, 2 * i + 1):
                            split_h2(c + 1, j)
                    for q, out in enumerate((gated, prod)):
                        act.wait_ge(S[("low_free", "high_free")[q]], 2 * (b + i + 1))
                        nc.scalar.activation(out[:], ft[:, 4 * i + 2 * q:4 * i + 2 * q + 2, :], ACT.Square)\
                            .then_inc(S["squared"], 1)
                        if q == i:
                            weights(b + i + 1, 1)
                act.wait_ge(S["sum_split"], c + 1)

            def down(b, part, c=None):
                def body(b, i):
                    weights(b, 0)
                    if part == 0:
                        for q in range(2):
                            act.wait_ge(S["doneB"], 2 * (b - 1) + q + 1)
                            copy(ft[:, DS(4 * i + 2 * q, 2), :].rearrange("p k n -> p (k n)"), pair(2 * q))\
                                .then_inc(S[("low_free", "high_free")[q]], 2)
                    weights(b, 1)

                if c is None:
                    with act.Fori(0, DN) as i:
                        body(b + i + 1, i)
                else:
                    body(b + 1, 0)
                    y_rows(c, NPLE - 1)
                    body(b + 2, 1)

            def x2_pairs(c, i):
                for q in range(2):
                    n = 2 * i + q
                    act.wait_ge(S["x2_ready"], c * 4 + n + 3)
                    copy(x2[:, 0, DS(2 * n, 2), :].rearrange("p k n -> p (k n)"),
                         ft[:, DS(2 * n, 2), :].rearrange("p k n -> p (k n)")).then_inc(S["x2_hi"], 1)

            def embedded_rows(c):
                act.wait_ge(S["sum_done"], c + 1)
                root(rnorm[:], ps[:, 6, :], D).then_inc(S["sum_root"], 1)
                act.wait_ge(S["pp_turned"], c + 1)
                copy(pturn[:, 0].rearrange("p k n -> p (k n)"), pair(4)).then_inc(S["pp_hi"], 1)

            def ple_body(b, c, i, last=False):
                if not last:
                    weights(b + 1, 0)
                for j in range(2):
                    act.wait_ge(S["doneA"], 2 * b + j + 1)
                    act.wait_ge(S["high_free"], 2 * b)
                    nc.scalar.activation(gated[:, j, :], ps[:, j, :], ACT.Sigmoid,
                                         bias=bgate[:, DS(2 * i + j)]).then_inc(S["low_free"], 1)

            def ple(b, c, end=False):
                ple_body(b, c, 0)
                weights(b + 1, 1)
                with act.Fori(1, NPLE - 1) as i:
                    ple_body(b + i, c, i)
                    y_rows(c, i - 1)
                    weights(b + i + 1, 1)
                ple_body(b + NPLE - 1, c, NPLE - 1, end)
                y_rows(c, NPLE - 2)
                if not end:
                    weights(b + NPLE, 1)

            def chunk(b, c, before, ahead=True):
                if before is None:
                    gate_ups(b, GU[0])
                    b = b + GU[0]
                else:
                    gate_up(b, 0)
                    embedded_rows(before)
                    with act.Fori(0, 2) as i:
                        x2_pairs(before, i)
                        gate_up(b + i + 1, 2 * i + 2)
                    gate_up(b + 3, 6)
                    b = b + GU[0]
                    ple(b, before)
                    b = b + NPLE
                down(b, 0, before)
                b = b + DN
                gate_ups(b, GU[1])
                down(b + GU[1], 1)
                b = b + GU[1] + DN
                gate_ups(b, GU[2])
                last_down(b + GU[2], c, ahead)

            weights(0, 0)
            for j in range(4):
                split_h2(0, j)
            weights(0, 1)
            act.wait_ge(S["memory_free"], 1)
            chunk(0, 0, None)
            with act.Fori(0, NCH - 2) as c:
                chunk(BODIES0 + c * BODIES, c + 1, c)
            chunk(BODIES0 + (NCH - 2) * BODIES, NCH - 1, NCH - 2, False)
            embedded_rows(NCH - 1)
            with act.Fori(0, 2) as i:
                x2_pairs(NCH - 1, i)
            ple(BODIES0 + (NCH - 1) * BODIES, NCH - 1, True)
            y_rows(NCH - 1, NPLE - 1)

        @block.vector
        def _(dve):
            step = Signal(S["step_v"])
            V = nc.vector

            def go(ins):
                step.by(ins)
                dve.wait_ge(step.sem, step.value)

            f = lambda ap: ap.bitcast(F32)

            dve.wait_ge(S["first_in"], 32)
            V.memset(ones[:].bitcast(F32), 1.0).then_inc(S["ones_set"], 1)
            V.memset(eps[:, 0:1], EPS)
            V.memset(eps[:, 1:2], HD * EPS).then_inc(S["eps_set"], 1)
            dve.wait_ge(S["pw_hi"], 1)
            go(V.tensor_tensor(poolw[:, 1].rearrange("p g n -> p (g n)"),
                               qtok[:].rearrange("p h d -> p (h d)"),
                               f(poolw[:, 0]).rearrange("p g n -> p (g n)"), ALU.subtract))

            def head_sums(src, h, done):
                a = tmp_a[:, 0:h, :]
                go(V.tensor_tensor(a, src, src, ALU.mult))
                V.tensor_reduce(small[:, 6:6 + h], a, AX.X, ALU.add).then_inc(done, 1)

            def head_norm_rope(src, h, gain, t, out, rooted, n):
                a, b, r = tmp_a[:, 0:h, :], tmp_b[:, 0:h, :], small[:, 6:6 + h]
                dve.wait_ge(rooted, n + 1)
                go(V.reciprocal(r, r))
                go(V.tensor_tensor(src, src, r.unsqueeze(2).to_broadcast([P, h, HD]), ALU.mult))
                go(V.tensor_tensor(src, src, gqk[:, gain:gain + 1, :].to_broadcast([P, h, HD]), ALU.mult))
                two = lambda ap: ap.rearrange("p h (d e) -> p h d e", e=2)
                row = lambda tb: tb[:, DS(t), :].unsqueeze(3).to_broadcast([P, h, HD // 2, 2])
                V.tensor_tensor(two(a), two(src), row(rope_c), ALU.mult)
                go(V.tensor_tensor(two(b), two(src), row(rope_s), ALU.mult))
                V.tensor_tensor(two(out)[:, :, :, 0], two(a)[:, :, :, 0], two(b)[:, :, :, 1], ALU.subtract)
                return V.tensor_tensor(two(out)[:, :, :, 1], two(b)[:, :, :, 0], two(a)[:, :, :, 1], ALU.add)

            def norm(n, s):
                dve.wait_ge(S["x_root"], n + 1)
                go(V.reciprocal(small[:, 2:3], small[:, s:s + 1]))
                dve.wait_ge(S["x_turned"], n)
                V.tensor_scalar(hrow[:], xs_a[:, s, :], small[:, 2:3], None, ALU.mult)\
                    .then_inc(S["h_ready"], 1)

            def turned_lo(n, s):
                dve.wait_ge(S["ht_hi"], n + 1)
                V.tensor_tensor(ht[:, s, 1].rearrange("p k n -> p (k n)"), pair(0),
                                f(ht[:, s, 0]).rearrange("p k n -> p (k n)"), ALU.subtract)\
                    .then_inc(S["ht_split"], 1)

            norm(0, 0)
            turned_lo(0, 0)
            with repeat(dve, NSEQ, {step: V_STEPS}) as g:
                stages[dve] = (g, 0)

                def strip(k):
                    dve.wait_ge(S["strip_hi"], g * 16 + k + 1)
                    if k < KT:
                        V.scalar_tensor_tensor(out=win[:, 1, k, :], in0=strip_place(k)[0],
                                               scalar=gin[:, k:k + 1], in1=f(win[:, 0, k, :]),
                                               op0=ALU.mult, op1=ALU.subtract).then_inc(S["strip_split"], 1)
                        return
                    kk = k - KT - 4
                    V.tensor_tensor(wout_b[:, 1, kk, :], strip_place(k)[0], f(wout_b[:, 0, kk, :]),
                                    ALU.subtract).then_inc(S["strip_split"], 1)

                def project(i, s, ahead, rows=True):
                    t = 2 * i + s
                    n = g * NT + t
                    dve.wait_ge(S["k_raw"], n + 1)
                    V.tensor_tensor(values[:, DS(t), :, 1, :].rearrange("p t k d -> p (t k) d"),
                                    ps[:, 4, KV_W:2 * KV_W].rearrange("p (k d) -> p k d", k=NKV),
                                    f(values[:, DS(t), :, 0, :]).rearrange("p t k d -> p (t k) d"),
                                    ALU.subtract).then_inc(S["v_split"], 1)
                    dve.wait_ge(S["q_rope"], n)
                    head_sums(ktok[:], NKV, S["k_sums"])
                    go(head_norm_rope(ktok[:], NKV, 1, t, ktok[:], S["k_root"], n))
                    dve.wait_ge(S["k_turned"], n)
                    wide = ktok[:].unsqueeze(2).to_broadcast([P, NKV, 2, HD])
                    go(V.tensor_copy(kstack[:, :, 0:2, :].bitcast(F32R), wide))
                    V.tensor_tensor(kstack[:, :, 2:4, :], wide, kstack[:, :, 0:2, :], ALU.subtract)\
                        .then_inc(S["k_stack"], 1)
                    if ahead:
                        turned_lo(n + 1, 1 - s)
                    if rows:
                        norm(n + 2, s)
                    dve.wait_ge(S["q_out"], n + 1)
                    head_sums(qtok[:], NH, S["q_sums"])
                    head_norm_rope(qtok[:], NH, 0, t, heads[:, DS(t)].rearrange("p t h d -> p (t h) d"),
                                   S["q_root"], n)\
                        .then_inc(S["q_rope"], 1)

                dve.wait_ge(S["x1_stored"], g * NT * 16)
                dve.wait_ge(S["h2_stored"], g * NT * 16)
                for k in range(KT):
                    strip(k)
                    if k == 5:
                        norm(g * NT + 1, 1)
                dve.wait_ge(consts_in, 16 * NCONST)
                with repeat(dve, NT // 2 - 1, {step: 2 * AB_STEPS}) as i:
                    project(i, 0, True)
                    project(i, 1, True)
                project(NT // 2 - 1, 0, True, rows=False)
                project(NT // 2 - 1, 1, False, rows=False)
                stage_end(dve)

                def row_max(s):
                    dve.wait_ge(S["score_done"], g * NSTEP + s + 1)
                    V.tensor_reduce(negmax[:, s:s + 1], pair(2 * (s % 2)), AX.X, ALU.max, negate=True)\
                        .then_inc(S["max_done"], 1)

                def o_parts(hc):
                    dve.wait_ge(S["o_added"], g * 2 * NH + hc)
                    dve.wait_ge(S["exp_done"], g * NSTEP + 4 * hc + 4)
                    go(V.reciprocal(recip[:], rowsum[:, 4 * hc:4 * hc + 4]))
                    dve.wait_ge(S["misc_done"], g * NMISC + MISC[("o", hc)] + 1)
                    for e in range(2):
                        last = V.tensor_tensor(
                            oparts[:, e], ps[:, 7, :].rearrange("p (t e d) -> p t e d", t=4, e=2)[:, :, e, :],
                            recip[:].unsqueeze(2).to_broadcast([P, 4, HD]), ALU.mult)
                    last.then_inc(S["misc_free"], 1)

                for half in range(2):
                    rows = heads[:, 4 * half:4 * half + 4, 0, :]
                    go(V.tensor_copy(qh[:, half, :, 0, :].bitcast(F32R), rows))
                    V.tensor_tensor(qh[:, half, :, 1, :], rows, qh[:, half, :, 0, :], ALU.subtract)\
                        .then_inc(S["qh_ready"], 1)
                row_max(0)
                row_max(1)
                for s in range(NSTEP):
                    h, u = s // NT, s % NT
                    if s + 2 < NSTEP:
                        row_max(s + 2)
                    for half in range(2):
                        dve.wait_ge(S["p_hi"], 2 * (g * NSTEP + s) + half + 1)
                        at = (slice(None), (s // 4) % 2, slice(None), slice(4 * half, 4 * half + 4),
                              slice((u % 4) * P, (u % 4 + 1) * P))
                        V.tensor_tensor(pt[at][:, 1], ps[:, 4 + half, :].rearrange("p (k n) -> p k n", k=4),
                                        f(pt[at][:, 0]), ALU.subtract).then_inc(S["p_split"], 1)
                    if u in (0, 4) and h:
                        o_parts(2 * h - 2 + u // 4)
                o_parts(2 * NH - 2)
                o_parts(2 * NH - 1)
                stage_end(dve)

                def concat_lo(t, s):
                    dve.wait_ge(S["c_hi"], g * NT + t + 1)
                    V.tensor_tensor(ct[:, s, 1, 0:4, :], chan[:, 0:NPOOL, PAD + t * P:PAD + (t + 1) * P],
                                    f(ct[:, s, 0, 0:4, :]), ALU.subtract)
                    V.tensor_tensor(ct[:, s, 1, 4:8, :], ps[:, 0, :].rearrange("p (k n) -> p k n", k=4),
                                    f(ct[:, s, 0, 4:8, :]), ALU.subtract).then_inc(S["c_split"], 1)

                def post_a(t):
                    n = g * NT + t
                    dve.wait_ge(S["m_root"], n + 1)
                    go(V.reciprocal(small[:, 6:7], small[:, 4:5]))
                    dve.wait_ge(S["x1_ready"], n)
                    V.scalar_tensor_tensor(out=mixn[:], in0=pair(1 + 2 * (t % 2)), scalar=small[:, 6:7],
                                           in1=gpost[:], op0=ALU.mult, op1=ALU.mult)\
                        .then_inc(S["mix_read"], 1)
                    dve.wait_ge(S[f"xd_in{t % 2}"], (g * (NT // 2) + t // 2 + 1) * 16)
                    dve.wait_ge(S["h2_ready"], n)
                    dve.wait_ge(S["x1_turned"], n)
                    dve.wait_ge(S["x1_root"], n)
                    dve.wait_ge(S["mix_read"], n + 1)
                    V.tensor_tensor(x1[:], mixn[:], xs_d[:, t % 2, :], ALU.add).then_inc(S["x1_ready"], 1)

                def post_b(t):
                    n = g * NT + t
                    dve.wait_ge(S["x1_root"], n + 1)
                    go(V.reciprocal(small[:, 7:8], small[:, 5:6]))
                    dve.wait_ge(S["h2_turned"], n)
                    V.scalar_tensor_tensor(out=h2[:], in0=x1[:], scalar=small[:, 7:8], in1=gffn[:],
                                           op0=ALU.mult, op1=ALU.mult).then_inc(S["h2_ready"], 1)

                concat_lo(0, 0)
                for k in range(KT + 4, 2 * KT):
                    strip(k)
                dve.wait_ge(S["gains_in"], 32 * (g + 1))
                for t in range(NT):
                    if t:
                        post_a(t - 1)
                    if t + 1 < NT:
                        concat_lo(t + 1, (t + 1) % 2)
                    if t:
                        post_b(t - 1)
                post_a(NT - 1)
                norm(g * NT + NT, 0)
                post_b(NT - 1)
                turned_lo(g * NT + NT, 0)
                stage_end(dve)

            def weights(b, sd):
                ab = "AB"[sd]
                for n, cut in enumerate(halves(sd)):
                    dve.wait_ge(S["hi" + ab], (2, 1)[sd] * b + n + 1)
                    V.tensor_tensor(wb[:, sd, 1, cut], rawb[sd][:, cut], f(wb[:, sd, 0, cut]),
                                    ALU.subtract).then_inc(S["split" + ab], 1)

            def gate_up(b, tile, tiles):
                weights(b + 1, 0)
                for j in range(2):
                    dve.wait_ge(S["low_free"], 2 * b + j + 1)
                    dve.wait_ge(S["doneB"], 2 * b + j + 1)
                    V.tensor_tensor(prod[:, j, :], gated[:, j, :], ps[:, 2 + j, :], ALU.mult)\
                        .then_inc(S["high_free"], 1)
                    dve.wait_ge(S["ff_hi"], tiles + j + 1)
                    V.tensor_tensor(ff[:, 1, DS(tile + j), :].rearrange("p k n -> p (k n)"), prod[:, j, :],
                                    f(ff[:, 0, DS(tile + j), :]).rearrange("p k n -> p (k n)"),
                                    ALU.subtract).then_inc(S["ff_split"], 1)
                weights(b + 1, 1)

            def gate_ups(b, times, tiles):
                with dve.Fori(0, times) as i:
                    gate_up(b + i, 2 * i, tiles + 2 * i)

            def add_rows(b, i, q):
                dve.wait_ge(S["doneB"], 2 * b + q + 1)
                rows = ft[:, DS(4 * i + 2 * q, 2), :].rearrange("p k n -> p (k n)")
                V.tensor_tensor(rows, rows, pair(2 * q), ALU.add)\
                    .then_inc(S[("low_free", "high_free")[q]], 2)

            def down(b, part):
                with dve.Fori(0, DN) as i:
                    weights(b + i + 1, 0)
                    if part:
                        for q in range(2):
                            add_rows(b + i, i, q)
                    weights(b + i + 1, 1)

            def split_h2(c, j):
                dve.wait_ge(S["h2_hi"], 4 * c + j + 1)
                V.tensor_tensor(h2c[:, 1, 2 * j:2 * j + 2], f(x2[:, 0, 2 * j:2 * j + 2]),
                                f(h2c[:, 0, 2 * j:2 * j + 2]), ALU.subtract).then_inc(S["h2_split"], 1)

            def last_down(b, c, ahead):
                go(V.memset(sumsq[:], 0.0))
                for i in range(DN):
                    weights(b + i + 1, 0)
                    if ahead:
                        for j in (2 * i, 2 * i + 1):
                            split_h2(c + 1, j)
                    for q in range(2):
                        add_rows(b + i, i, q)
                    if i == 0:
                        weights(b + i + 1, 1)
                    for q, squares in enumerate((gated, prod)):
                        dve.wait_ge(S["squared"], 4 * c + 2 * i + q + 1)
                        for j in range(2):
                            go(V.tensor_tensor(sumsq[:], sumsq[:], squares[:, j], ALU.add))
                go(V.tensor_copy(sumhl[:, 0, :], sumsq[:]))
                V.tensor_tensor(sumhl[:, 1, :], sumsq[:], f(sumhl[:, 0, :]), ALU.subtract)\
                    .then_inc(S["sum_split"], 1)
                weights(b + DN, 1)

            def token_sums(c):
                dve.wait_ge(S["sum_root"], c + 1)
                go(V.reciprocal(rnorm[:], rnorm[:]))
                alone(dve)

            def embedded_rows(c):
                dve.wait_ge(S["pp_hi"], c + 1)
                V.tensor_tensor(pturn[:, 1].rearrange("p k n -> p (k n)"), pair(4),
                                f(pturn[:, 0]).rearrange("p k n -> p (k n)"), ALU.subtract)\
                    .then_inc(S["pp_split"], 1)

            def x2_pairs(c, i):
                for q in range(2):
                    n = 2 * i + q
                    if q:
                        dve.wait_ge(S["x2_ready"], c * 4 + n + 2)
                    for j in range(2):
                        last = V.scalar_tensor_tensor(
                            out=sqs[:, j, :], in0=ft[:, DS(2 * n + j), :].rearrange("p k n -> p (k n)"),
                            scalar=gpost2[:, DS(2 * n + j)], in1=rnorm[:], op0=ALU.mult, op1=ALU.mult)
                    go(last)
                    dve.wait_ge(S[f"xres{q}"], 16 * (c * 2 + i + 1))
                    V.tensor_tensor(ft[:, DS(2 * n, 2), :], sqs[:], xres[:, q], ALU.add)\
                        .then_inc(S["x2_ready"], 1)
                for q in range(2):
                    n = 2 * i + q
                    dve.wait_ge(S["x2_hi"], c * 4 + n + 1)
                    V.tensor_tensor(x2[:, 1, DS(2 * n, 2), :], ft[:, DS(2 * n, 2), :],
                                    f(x2[:, 0, DS(2 * n, 2), :]), ALU.subtract).then_inc(S["x2_split"], 1)

            def ple(b, c, end=False):
                def body(b, i, last):
                    if not last:
                        weights(b + 1, 0)
                    for j in range(2):
                        dve.wait_ge(S["low_free"], 2 * b + j + 1)
                        dve.wait_ge(S["doneB"], 2 * b + j + 1)
                        V.tensor_tensor(prod[:, j, :], gated[:, j, :], ps[:, 2 + j, :], ALU.mult)\
                            .then_inc(S["high_free"], 1)
                    dve.wait_ge(S["high_free"], 2 * b + 2)
                    rows = ft[:, DS(2 * i, 2), :]
                    V.tensor_tensor(rows, rows, prod[:], ALU.add).then_inc(S["y_ready"], 1)
                    if not last:
                        weights(b + 1, 1)

                with dve.Fori(0, NPLE - 1) as i:
                    body(b + i, i, False)
                body(b + NPLE - 1, NPLE - 1, end)

            def chunk(b, c, before, ahead=True):
                tiles = c * NHID
                if before is None:
                    gate_ups(b, GU[0], tiles)
                    b = b + GU[0]
                else:
                    gate_up(b, 0, tiles)
                    token_sums(before)
                    with repeat(dve, 2, {step: 2}) as i:
                        x2_pairs(before, i)
                        gate_up(b + i + 1, 2 * i + 2, tiles + 2 * i + 2)
                    embedded_rows(before)
                    gate_up(b + 3, 6, tiles + 6)
                    b = b + GU[0]
                    ple(b, before)
                    b = b + NPLE
                down(b, 0)
                b = b + DN
                gate_ups(b, GU[1], tiles + PART0[1])
                down(b + GU[1], 1)
                b = b + GU[1] + DN
                gate_ups(b, GU[2], tiles + PART0[2])
                last_down(b + GU[2], c, ahead)

            dve.sem_inc(S["x2_ready"], 2)
            weights(0, 0)
            for j in range(4):
                split_h2(0, j)
            weights(0, 1)
            chunk(0, 0, None)
            with repeat(dve, NCH - 2, {step: 15}) as c:
                chunk(BODIES0 + c * BODIES, c + 1, c)
            chunk(BODIES0 + (NCH - 2) * BODIES, NCH - 1, NCH - 2, False)
            token_sums(NCH - 1)
            with repeat(dve, 2, {step: 2}) as i:
                x2_pairs(NCH - 1, i)
            embedded_rows(NCH - 1)
            ple(BODIES0 + (NCH - 1) * BODIES, NCH - 1, True)


def rope_tables():
    t = np.arange(SEQ)
    row, col = (t // GRID_W).astype(np.float32), (t % GRID_W).astype(np.float32)
    ax = HD // 2
    inv = (1.0 / (np.float32(ROPE_THETA) ** (np.arange(0, ax, 2, dtype=np.float32) / np.float32(ax))))
    inv = inv.astype(np.float32)
    ang = np.concatenate([row[:, None] * inv, col[:, None] * inv], axis=-1).astype(np.float32)
    lay = lambda a: np.ascontiguousarray(a.reshape(NT, P, HD // 2).transpose(1, 0, 2).astype(np.float32))
    return lay(np.cos(ang)), lay(np.sin(ang))


def edge_table():
    out = np.ones((NPOOL, 2, PAD), np.float32)
    for n, w in enumerate(WINDOWS):
        for side, t0 in enumerate((0, SEQ - PAD)):
            t = np.arange(t0, t0 + PAD)
            held = np.clip(t + w - 1 - w // 2, 0, SEQ - 1) - np.clip(t - w // 2, 0, SEQ - 1) + 1
            out[n, side] = w / held
    return out


def kernel(x_prompt, x_sample, p_prompt, p_sample, ln_mix_pre, ln_mix_post, w_in, pool_w, pool_scale,
           q_norm, k_norm, w_out, ln_ffn_pre, ln_ffn_post, w_gate, w_up, w_down,
           w_ple_proj, w_ple_gate, b_ple_gate):
    import concourse.bacc as bacc
    from concourse.bass_utils import run_bass_kernel_spmd

    nc = bacc.Bacc("TRN2", target_bir_lowering=False, num_devices=1)
    cos, sin = rope_tables()
    rows = lambda a, b, n: np.concatenate([np.asarray(a).reshape(NT, P, n), np.asarray(b).reshape(NT, P, n)])
    arrays = {
        "x": rows(x_prompt, x_sample, D), "p": rows(p_prompt, p_sample, PLE),
        "ident_d": np.eye(P, dtype=np.float32), "cos_d": cos, "sin_d": sin, "edge_d": edge_table(),
        "g_mix_pre": ln_mix_pre[0], "g_mix_post": ln_mix_post[0], "w_in": w_in[0], "pool_w": pool_w[0],
        "pool_scale": pool_scale[0], "q_norm": q_norm[0], "k_norm": k_norm[0], "w_out": w_out[0],
        "g_ffn_pre": ln_ffn_pre[0], "g_ffn_post": ln_ffn_post[0], "w_gate": w_gate[0], "w_up": w_up[0],
        "w_down": w_down[0], "w_proj": w_ple_proj[0], "w_pgate": w_ple_gate[0], "b_pgate": b_ple_gate[0],
    }
    arrays = {"in_" + k: np.ascontiguousarray(a) for k, a in arrays.items()}
    args = {k[3:]: nc.dram_tensor(k, a.shape, mybir.dt.from_np(a.dtype), kind="ExternalInput").ap()
            for k, a in arrays.items()}
    y = nc.dram_tensor("y", (NSEQ * NT, P, D), F32, kind="ExternalOutput").ap()
    encoder_layer(nc, **args, y=y)
    got = run_bass_kernel_spmd(nc, [arrays], core_ids=[0]).results[0]["y"]
    return tuple(got.reshape(NSEQ, 1, SEQ, D))
```
